# Optimizing a Trainium2 kernel written in Bass

```python
import jax, jax.numpy as jnp
from jax import lax
import numpy as np

D_MODEL = 1024
BATCH = 1
SEQ = 1024
DEPTH = 1

CHUNK = 64
N_MIXERS = 4
EPS = 1e-6
D_FF = 2816
NEG_INF = -1e30

HGRN_HEADS = 8
HGRN_HEAD_DIM = D_MODEL // HGRN_HEADS

GLA_HEADS = 4
GLA_KEY_DIM = D_MODEL // 2
GLA_VALUE_DIM = D_MODEL
GLA_HEAD_K = GLA_KEY_DIM // GLA_HEADS
GLA_HEAD_V = GLA_VALUE_DIM // GLA_HEADS
GLA_GATE_RANK = 16
GLA_GATE_NORMALIZER = 16.0

ATTN_HEADS = 16
ATTN_HEAD_DIM = D_MODEL // ATTN_HEADS
LEFT_CHUNKS = 8
BAND = (LEFT_CHUNKS + 1) * CHUNK
REL_CLIP = 2 * CHUNK
N_REL = REL_CLIP + CHUNK

LRU_WIDTH = D_MODEL
LRU_HEADS = 4
LRU_BLOCK = LRU_WIDTH // LRU_HEADS
CONV_WIDTH = 4
LRU_C = 8.0

kernel_name = 'hybrid_chunk_causal_encoder'

def rms_norm(x, gain):
    xf = x.astype(jnp.float32)
    y = xf * lax.rsqrt(jnp.mean(xf * xf, axis=-1, keepdims=True) + EPS)
    return (y * gain.astype(jnp.float32)).astype(x.dtype)

def swiglu(h, w_gate_up, w_down):
    g, u = jnp.split(h @ w_gate_up, 2, axis=-1)
    return (jax.nn.silu(g) * u) @ w_down

def split_heads(t, n_heads):
    b, l, _ = t.shape
    return t.reshape(b, l, n_heads, -1).transpose(0, 2, 1, 3)

def merge_heads(t):
    b, h, l, d = t.shape
    return t.transpose(0, 2, 1, 3).reshape(b, l, h * d)

def chunk_gated_linear_attention(q, k, v, log_f, scale):
    b, h, l, dk = q.shape
    dv = v.shape[-1]
    n = l // CHUNK
    out_dtype = v.dtype

    def to_chunks(t):
        t = t.astype(jnp.float32)
        return jnp.moveaxis(t.reshape(b, h, n, CHUNK, t.shape[-1]), 2, 0)

    qc, kc, vc, gc = to_chunks(q * scale), to_chunks(k), to_chunks(v), to_chunks(log_f)
    causal = jnp.tril(jnp.ones((CHUNK, CHUNK), dtype=bool))

    def step(state, inp):
        q_i, k_i, v_i, g_i = inp
        cum = jnp.cumsum(g_i, axis=-2)
        rel = cum[..., :, None, :] - cum[..., None, :, :]
        decay = jnp.exp(jnp.where(causal[:, :, None], rel, -jnp.inf))
        scores = jnp.einsum('bhtk,bhsk,bhtsk->bhts', q_i, k_i, decay)
        o = (jnp.einsum('bhts,bhsv->bhtv', scores, v_i)
             + jnp.einsum('bhtk,bhkv->bhtv', q_i * jnp.exp(cum), state))
        last = cum[..., -1:, :]
        state = (jnp.exp(last[..., 0, :])[..., None] * state
                 + jnp.einsum('bhsk,bhsv->bhkv', k_i * jnp.exp(last - cum), v_i))
        return state, o

    s0 = jnp.zeros((b, h, dk, dv), jnp.float32)
    _, o = lax.scan(step, s0, (qc, kc, vc, gc))
    return jnp.moveaxis(o, 0, 2).reshape(b, h, l, dv).astype(out_dtype)

def hgrn2_mixer(h, w_in, lower_bound, norm_gain, w_out):
    q, f, i, g = jnp.split(h @ w_in, 4, axis=-1)
    q = jax.nn.silu(q)
    fgate = lower_bound + (1.0 - lower_bound) * jax.nn.sigmoid(f.astype(jnp.float32))
    k = 1.0 - fgate
    log_f = jnp.log(fgate)
    o = chunk_gated_linear_attention(split_heads(q, HGRN_HEADS), split_heads(k, HGRN_HEADS),
                                     split_heads(i, HGRN_HEADS), split_heads(log_f, HGRN_HEADS),
                                     HGRN_HEAD_DIM ** -0.5)
    o = merge_heads(rms_norm(o, norm_gain)) * jax.nn.silu(g)
    return o @ w_out

def gla_mixer(h, w_in, w_gate_down, w_gate_up, gate_bias, norm_gain, w_out):
    q, k, v, g = jnp.split(h @ w_in, [GLA_KEY_DIM, 2 * GLA_KEY_DIM, 2 * GLA_KEY_DIM + GLA_VALUE_DIM], axis=-1)
    gate_logits = ((h @ w_gate_down) @ w_gate_up + gate_bias).astype(jnp.float32)
    log_f = jax.nn.log_sigmoid(gate_logits) / GLA_GATE_NORMALIZER
    o = chunk_gated_linear_attention(split_heads(q, GLA_HEADS), split_heads(k, GLA_HEADS),
                                     split_heads(v, GLA_HEADS), split_heads(log_f, GLA_HEADS),
                                     GLA_HEAD_K ** -0.5)
    o = merge_heads(rms_norm(o, norm_gain)) * jax.nn.silu(g)
    return o @ w_out

def chunked_relbias_attention(h, w_qkv, rel_table, w_out):
    b, l, _ = h.shape
    n = l // CHUNK
    pad = BAND - CHUNK
    q, k, v = jnp.split(h @ w_qkv, 3, axis=-1)
    q = split_heads(q * ATTN_HEAD_DIM ** -0.5, ATTN_HEADS)
    k = split_heads(k, ATTN_HEADS)
    v = split_heads(v, ATTN_HEADS)
    kp = jnp.pad(k, ((0, 0), (0, 0), (pad, 0), (0, 0)))
    vp = jnp.pad(v, ((0, 0), (0, 0), (pad, 0), (0, 0)))
    dist = jnp.arange(CHUNK)[:, None] + pad - jnp.arange(BAND)[None, :]
    rel_idx = jnp.clip(dist, -(CHUNK - 1), REL_CLIP) + (CHUNK - 1)
    bias = rel_table.astype(jnp.float32)[:, rel_idx]
    qc = jnp.moveaxis(q.reshape(b, ATTN_HEADS, n, CHUNK, ATTN_HEAD_DIM), 2, 0)

    def one_chunk(args):
        c, q_c = args
        start = c * CHUNK
        k_band = lax.dynamic_slice_in_dim(kp, start, BAND, axis=2)
        v_band = lax.dynamic_slice_in_dim(vp, start, BAND, axis=2)
        scores = jnp.einsum('bhtd,bhsd->bhts', q_c, k_band).astype(jnp.float32) + bias
        key_pos = start - pad + jnp.arange(BAND)
        scores = jnp.where(key_pos >= 0, scores, NEG_INF)
        p = jax.nn.softmax(scores, axis=-1).astype(v_band.dtype)
        return jnp.einsum('bhts,bhsd->bhtd', p, v_band)

    o = lax.map(one_chunk, (jnp.arange(n), qc))
    o = jnp.moveaxis(o, 0, 2).reshape(b, ATTN_HEADS, l, ATTN_HEAD_DIM)
    return merge_heads(o) @ w_out

def causal_depthwise_conv(x, w, bias):
    y = lax.conv_general_dilated(x, w[:, None, :].astype(x.dtype), window_strides=(1,),
                                 padding=[(CONV_WIDTH - 1, 0)],
                                 dimension_numbers=('NWC', 'WIO', 'NWC'),
                                 feature_group_count=x.shape[-1])
    return y + bias

def _linear_combine(left, right):
    a1, b1 = left
    a2, b2 = right
    return a1 * a2, a2 * b1 + b2

def rg_lru(x, w_a, b_a, w_x, b_x, lam):
    b, l, w = x.shape
    xf = x.astype(jnp.float32)
    xh = xf.reshape(b, l, LRU_HEADS, LRU_BLOCK)
    r = jax.nn.sigmoid(jnp.einsum('blhi,hij->blhj', xh, w_a.astype(jnp.float32)).reshape(b, l, w) + b_a)
    i = jax.nn.sigmoid(jnp.einsum('blhi,hij->blhj', xh, w_x.astype(jnp.float32)).reshape(b, l, w) + b_x)
    log_a = -LRU_C * r * jax.nn.softplus(-lam.astype(jnp.float32))
    a = jnp.exp(log_a)
    mult = jnp.sqrt(-jnp.expm1(2.0 * log_a))
    mult = mult.at[:, 0].set(1.0)
    _, hs = lax.associative_scan(_linear_combine, (a, mult * i * xf), axis=1)
    return hs.astype(x.dtype)

def rglru_mixer(h, w_in, conv_w, conv_b, w_a, b_a, w_x, b_x, lam, w_out):
    y, xb = jnp.split(h @ w_in, 2, axis=-1)
    y = jax.nn.gelu(y, approximate=True)
    xb = causal_depthwise_conv(xb, conv_w, conv_b)
    hr = rg_lru(xb, w_a, b_a, w_x, b_x, lam)
    return (y * hr) @ w_out

def setup_inputs(seed: int = 0) -> dict:
    key = jax.random.key(seed)
    keys = iter(jax.random.split(key, 32))

    def normal(shape, scale):
        return scale * jax.random.normal(next(keys), shape, jnp.float32)

    n_a, n_b, n_c, n_d = [len(range(m, DEPTH, N_MIXERS)) for m in range(N_MIXERS)]
    d = D_MODEL
    a0 = jax.random.uniform(next(keys), (n_d, LRU_WIDTH), jnp.float32, minval=0.9, maxval=0.999)
    return {
        'x': normal((BATCH, SEQ, d), 1.0),
        'ffn_w_gate_up': normal((DEPTH, 2, d, 2 * D_FF), d ** -0.5),
        'ffn_w_down': normal((DEPTH, 2, D_FF, d), D_FF ** -0.5),
        'norm_gains': 1.0 + normal((DEPTH, 3, d), 0.02),
        'final_norm_gain': 1.0 + normal((d,), 0.02),
        'hgrn_w_in': normal((n_a, d, 4 * d), d ** -0.5),
        'hgrn_lower_bound_logits': normal((DEPTH + 1, d), 0.5),
        'hgrn_norm_gain': 1.0 + normal((n_a, HGRN_HEAD_DIM), 0.02),
        'hgrn_w_out': normal((n_a, d, d), d ** -0.5),
        'gla_w_in': normal((n_b, d, 2 * GLA_KEY_DIM + 2 * GLA_VALUE_DIM), d ** -0.5),
        'gla_w_gate_down': normal((n_b, d, GLA_GATE_RANK), d ** -0.5),
        'gla_w_gate_up': normal((n_b, GLA_GATE_RANK, GLA_KEY_DIM), GLA_GATE_RANK ** -0.5),
        'gla_gate_bias': normal((n_b, GLA_KEY_DIM), 0.1),
        'gla_norm_gain': 1.0 + normal((n_b, GLA_HEAD_V), 0.02),
        'gla_w_out': normal((n_b, GLA_VALUE_DIM, d), GLA_VALUE_DIM ** -0.5),
        'attn_w_qkv': normal((n_c, d, 3 * d), d ** -0.5),
        'attn_rel_bias': normal((n_c, ATTN_HEADS, N_REL), 0.1),
        'attn_w_out': normal((n_c, d, d), d ** -0.5),
        'lru_w_in': normal((n_d, d, 2 * LRU_WIDTH), d ** -0.5),
        'lru_conv_w': normal((n_d, CONV_WIDTH, LRU_WIDTH), CONV_WIDTH ** -0.5),
        'lru_conv_b': normal((n_d, LRU_WIDTH), 0.02),
        'lru_w_a': normal((n_d, LRU_HEADS, LRU_BLOCK, LRU_BLOCK), LRU_BLOCK ** -0.5),
        'lru_b_a': normal((n_d, LRU_WIDTH), 0.02),
        'lru_w_x': normal((n_d, LRU_HEADS, LRU_BLOCK, LRU_BLOCK), LRU_BLOCK ** -0.5),
        'lru_b_x': normal((n_d, LRU_WIDTH), 0.02),
        'lru_lambda': jnp.log(a0) - jnp.log1p(-a0),
        'lru_w_out': normal((n_d, LRU_WIDTH, d), LRU_WIDTH ** -0.5),
    }

def reference(x, ffn_w_gate_up, ffn_w_down, norm_gains, final_norm_gain,
              hgrn_w_in, hgrn_lower_bound_logits, hgrn_norm_gain, hgrn_w_out,
              gla_w_in, gla_w_gate_down, gla_w_gate_up, gla_gate_bias, gla_norm_gain, gla_w_out,
              attn_w_qkv, attn_rel_bias, attn_w_out,
              lru_w_in, lru_conv_w, lru_conv_b, lru_w_a, lru_b_a, lru_w_x, lru_b_x, lru_lambda, lru_w_out):
    lower_bounds = jnp.cumsum(jax.nn.softmax(hgrn_lower_bound_logits.astype(jnp.float32), axis=0), axis=0)
    for i in range(DEPTH):
        m, j = i % N_MIXERS, i // N_MIXERS
        x = x + 0.5 * swiglu(rms_norm(x, norm_gains[i, 0]), ffn_w_gate_up[i, 0], ffn_w_down[i, 0])
        h = rms_norm(x, norm_gains[i, 1])
        if m == 0:
            y = hgrn2_mixer(h, hgrn_w_in[j], lower_bounds[i], hgrn_norm_gain[j], hgrn_w_out[j])
        elif m == 1:
            y = gla_mixer(h, gla_w_in[j], gla_w_gate_down[j], gla_w_gate_up[j], gla_gate_bias[j],
                          gla_norm_gain[j], gla_w_out[j])
        elif m == 2:
            y = chunked_relbias_attention(h, attn_w_qkv[j], attn_rel_bias[j], attn_w_out[j])
        else:
            y = rglru_mixer(h, lru_w_in[j], lru_conv_w[j], lru_conv_b[j], lru_w_a[j], lru_b_a[j],
                            lru_w_x[j], lru_b_x[j], lru_lambda[j], lru_w_out[j])
        x = x + y
        x = x + 0.5 * swiglu(rms_norm(x, norm_gains[i, 2]), ffn_w_gate_up[i, 1], ffn_w_down[i, 1])
    return rms_norm(x, final_norm_gain)


_drawn_inputs = setup_inputs


def setup_inputs(seed=0):
    import zlib

    import numpy as np

    out = dict(_drawn_inputs(seed))
    spreads = {}
    factors = {'norm_gains': 3.004, 'final_norm_gain': 2.703, 'hgrn_norm_gain': 5.301}
    for name, (base, spread) in spreads.items():
        noise = np.random.default_rng([zlib.crc32(name.encode()), seed]).standard_normal(out[name].shape)
        drawn = base * np.exp(spread * noise) if base else spread * noise
        out[name] = __import__('jax').numpy.asarray(drawn.astype(out[name].dtype))
    for name, factor in factors.items():
        out[name] = (out[name] * factor).astype(out[name].dtype)
    return out
```

```python
from contextlib import ExitStack

import concourse.bass as bass
from concourse import mybir

F32 = mybir.dt.float32
F32R = mybir.dt.float32r
U32 = mybir.dt.uint32
ALU = mybir.AluOpType
ACT = mybir.ActivationFunctionType

P = 128
T = 1024
HALF = 512
D = 1024
DT = D // P
FF = 2816
FT = FF // P
GROUPS = FT // 2
HEADS = 8
NC = T // P
LEVELS = (64, 32, 16, 8, 4, 2, 1)
NL = len(LEVELS)
HD = D // HEADS
QSCALE = float(HD) ** -0.5
EPS = 1e-6
V_NORM, V_FINAL, V_LOGIT0, V_LOGIT1, V_HEAD = 0, 3 * DT, 4 * DT, 5 * DT, 6 * DT
NVEC = V_HEAD + 1
L_MAX, L_E0, L_E1, L_SUM, L_INV, L_LB, L_ONE_MINUS, L_MINUS = range(8)
TINY = 2.0 ** -60


def hgrn2_trunk(nc, x, w_gate_up, w_down, norm_gains, final_gain, w_in, lb_logits, head_gain,
                w_out, out):
    ctx = ExitStack()
    with ctx:
        def sb(stack, name, shape, dt=F32):
            return stack.enter_context(nc.sbuf_tensor(name, shape, dt))

        def sem(name):
            return ctx.enter_context(nc.semaphore(name))

        h_hi = sb(ctx, "h_hi", [P, DT, T], F32R)
        h_lo = sb(ctx, "h_lo", [P, DT, T], F32R)
        col_hi = sb(ctx, "col_hi", [P, 2, DT, P], F32R)
        col_lo = sb(ctx, "col_lo", [P, 2, DT, P], F32R)
        col_raw = sb(ctx, "col_raw", [P, 4, DT, P])
        ident = sb(ctx, "ident", [P, P])
        ones = sb(ctx, "ones", [P, P])
        masks = sb(ctx, "masks", [P, NL, P // 2])
        gains = sb(ctx, "gains", [P, NVEC])
        lbv = sb(ctx, "lbv", [P, 8, HEADS])
        vec_rows = sb(ctx, "vec_rows", [NVEC, P])
        eps = sb(ctx, "eps", [P, 1])

        ffn_mem = ExitStack()
        xT = sb(ffn_mem, "xT", [P, DT, T])
        sumsq = sb(ffn_mem, "sumsq", [P, T])
        rstd = sb(ffn_mem, "rstd", [P, T])
        act_hi = sb(ffn_mem, "act_hi", [P, 2, T], F32R)
        act_lo = sb(ffn_mem, "act_lo", [P, 2, T], F32R)
        row_hi = sb(ffn_mem, "row_hi", [P, 2, D], F32R)
        row_lo = sb(ffn_mem, "row_lo", [P, 2, D], F32R)
        row_raw = sb(ffn_mem, "row_raw", [P, 2, D])
        silu_g = sb(ffn_mem, "silu_g", [P, T])
        prod = sb(ffn_mem, "prod", [P, T])
        stage = sb(ffn_mem, "stage", [P, 4, D])
        ffn_mem.close()

        mix_mem = ExitStack()
        og = sb(mix_mem, "og", [P, HEADS, T])
        sig_a = sb(mix_mem, "sig_a", [P, T])
        sig_q = sb(mix_mem, "sig_q", [P, T])
        logf = sb(mix_mem, "logf", [P, T])
        cum = sb(mix_mem, "cum", [P, T])
        k_t = sb(mix_mem, "k_t", [P, T])
        q_t = sb(mix_mem, "q_t", [P, T])
        decay = sb(mix_mem, "decay", [P, 2, T])
        k_dec = sb(mix_mem, "k_dec", [P, 2, T])
        q_dec = sb(mix_mem, "q_dec", [P, 2, HALF])
        q_cum = sb(mix_mem, "q_cum", [P, T])
        k_end = sb(mix_mem, "k_end", [P, T])
        k_nat = sb(mix_mem, "k_nat", [P, NC, P])
        v_t = sb(mix_mem, "v_t", [P, T])
        v_nat = sb(mix_mem, "v_nat", [P, NC, P])
        scores = sb(mix_mem, "scores", [P, T])
        state = sb(mix_mem, "state", [P, NC, P])
        tile_dec = sb(mix_mem, "tile_dec", [P, NC])
        mix_mem.close()

        bank = [ctx.enter_context(nc.psum_tensor(f"bank{i}", [P, T], F32)) for i in range(4)]

        x_park = nc.dram_tensor("x_park", (P, DT * T), F32, kind="Internal").ap()

        block = ctx.enter_context(nc.Block())

        s_xload = [sem(f"x_rows_loaded{i}") for i in range(4)]
        s_vec = sem("vectors_loaded")
        s_ident = sem("identity_steps")
        s_ones = sem("ones_made")
        s_mask = sem("mask_steps")
        s_eps = sem("eps_made")
        s_turned = sem("x_tiles_turned")
        s_placed = [sem("x_placed_by_vector"), sem("x_placed_by_scalar")]
        s_vturn = sem("vectors_turned")
        s_gains = sem("gains_placed")
        s_lb = sem("lower_bound_steps")
        s_lbexp = sem("lower_bound_exps")
        s_cload = [sem(f"col_loaded{i}") for i in range(4)]
        s_chi = sem("col_hi_made")
        s_clo = sem("col_lo_made")
        s_cdone = sem("col_units_done")
        s_park = sem("x_parked")
        s_back = [sem(f"x_back{d}") for d in range(DT)]
        s_outturn = sem("out_tiles_turned")
        s_placed_out = [sem("out_rows_by_vector"), sem("out_rows_by_scalar")]
        s_out = [sem(f"rows_written{i}") for i in range(4)]

        class Norm:

            def __init__(self, tag):
                self.squared = sem(f"{tag}_squared")
                self.added = sem(f"{tag}_added")
                self.summed = sem(f"{tag}_summed")
                self.log = sem(f"{tag}_log")
                self.rstd = sem(f"{tag}_rstd")
                self.scaled = sem(f"{tag}_scaled")
                self.hi = sem(f"{tag}_hi")
                self.lo = sem(f"{tag}_lo")

        class Ffn:
            def __init__(self, tag, which, slot0, norm):
                self.which, self.slot0, self.norm = which, slot0, norm
                self.rload = [sem(f"{tag}_row_loaded{i}") for i in range(2)]
                self.rhi = sem(f"{tag}_row_hi_made")
                self.rlo = sem(f"{tag}_row_lo_made")
                self.silu = sem(f"{tag}_silu_made")
                self.prod = sem(f"{tag}_prod_made")
                self.ahi = sem(f"{tag}_act_hi_made")
                self.alo = sem(f"{tag}_act_lo_made")
                self.down = sem(f"{tag}_down_done")
                self.xadd = sem(f"{tag}_x_added")

        norms = [Norm(f"norm{i}") for i in range(4)]
        MIX0 = 4 * GROUPS
        OUT0 = MIX0 + 4 * HEADS
        FFN0 = OUT0 + DT
        SLOTS = FFN0 + 4 * GROUPS
        ffn_a = Ffn("ffn_a", 0, 0, norms[0])
        ffn_b = Ffn("ffn_b", 1, FFN0, norms[2])

        m_sigf = sem("m_sigmoid_f")
        m_logf = sem("m_log_f")
        m_k = sem("m_k_made")
        m_cum = sem("m_cum_made")
        m_tdec = sem("m_tile_decay")
        m_sigq = sem("m_sigmoid_q")
        m_q = sem("m_q_made")
        m_vt = sem("m_v_copied")
        m_sigg = sem("m_sigmoid_g")
        m_og = sem("m_out_gate")
        m_dif = sem("m_exponent_made")
        m_exp = sem("m_decay_made")
        m_ops = sem("m_decayed_operands")
        m_lvl = sem("m_level_scored")
        m_sel = sem("m_level_selected")
        m_vturn = sem("m_v_turned")
        m_vnat = sem("m_v_rows")
        m_kturn = sem("m_k_turned")
        m_knat = sem("m_k_rows")
        m_qexp = sem("m_exp_cum")
        m_qcum = sem("m_q_cum")
        m_upd = sem("m_state_products")
        m_state = sem("m_state_steps")
        m_o = sem("m_o_done")
        m_osq = sem("m_o_squared")
        m_osum = sem("m_o_summed")
        m_hlog = sem("m_head_log")
        m_hrstd = sem("m_head_rstd")
        m_norm = sem("m_o_normed")
        m_gated = sem("m_gated")
        m_zero = sem("m_buffers_zeroed")
        m_seen = sem("m_level_wait_passed")
        s_seen = sem("load_wait_passed")
        g_hi = sem("gated_hi_made")
        g_lo = sem("gated_lo_made")
        o_add = sem("mixer_x_added")

        def addr(eng, value):
            return value if isinstance(value, int) else eng.snap(value)

        def load_col(eng, src, n, r, started=True, alone=False):
            if started:
                eng.wait_ge(s_clo, n - 3)
            if alone:
                eng.sem_inc(s_seen, 1)
            eng.dma_start(col_raw[:, r], src.rearrange("(k p) c -> p k c", p=P)).then_inc(s_cload[r], 16)

        def split_hi_col(eng, n, r, started=True):
            eng.wait_ge(s_cload[r], (n - r) * 4 + 16)
            if started:
                eng.wait_ge(s_cdone, n - 1)
            eng.activation(col_hi[:, r % 2], col_raw[:, r], ACT.Copy).then_inc(s_chi, 1)

        def split_lo_col(eng, n, r):
            eng.wait_ge(s_chi, n + 1)
            eng.tensor_tensor(col_lo[:, r % 2], col_raw[:, r], col_hi[:, r % 2].bitcast(F32),
                              ALU.subtract).then_inc(s_clo, 1)

        def pe_three(eng, dst, w_hi, w_lo, a_hi, a_lo, first, last):
            for n, a in enumerate((a_hi, a_lo)):
                for c in range(2):
                    s = slice(c * HALF, (c + 1) * HALF)
                    eng.matmul(dst[:, s], w_hi, a[:, s], start=first and n == 0, stop=False)
            for c in range(2):
                s = slice(c * HALF, (c + 1) * HALF)
                mm = eng.matmul(dst[:, s], w_lo, a_hi[:, s], start=False, stop=last)
            return mm

        def pe_col_unit(eng, n, r, dst, h_ready=None, between=None):
            eng.wait_ge(s_clo, n + 1)
            for k in range(DT):
                if h_ready:
                    eng.wait_ge(h_ready, k + 1)
                mm = pe_three(eng, dst, col_hi[:, r % 2, k], col_lo[:, r % 2, k],
                              h_hi[:, k], h_lo[:, k], k == 0, k == DT - 1)
                if k == DT - 1:
                    mm.then_inc(s_cdone, 1)
                if between:
                    between(k)

        sq_buf = (silu_g, prod)

        def act_square(eng, nm, d, ready, count):
            eng.wait_ge(ready, count)
            if d >= 2:
                eng.wait_ge(nm.added, d - 1)
            eng.activation(sq_buf[d % 2][:], xT[:, d], ACT.Square).then_inc(nm.squared, 1)

        def dve_add_square(eng, nm, d):
            eng.wait_ge(nm.squared, d + 1)
            if d:
                eng.wait_ge(nm.added, d)
                eng.tensor_tensor(sumsq[:], sumsq[:], sq_buf[d % 2][:], ALU.add).then_inc(nm.added, 1)
            else:
                eng.tensor_copy(sumsq[:], sq_buf[0][:]).then_inc(nm.added, 1)

        def pe_norm_sum(eng, nm, dst):
            eng.wait_ge(nm.added, DT)
            for c in range(2):
                s = slice(c * HALF, (c + 1) * HALF)
                mm = eng.matmul(dst[:, s], ones[:], sumsq[:, s], start=True, stop=True)
            mm.then_inc(nm.summed, 1)

        def act_rstd(eng, nm, src):
            eng.wait_ge(nm.summed, 1)
            eng.activation(rstd[:], src[:], ACT.Ln, bias=eps[:], scale=1.0 / D).then_inc(nm.log, 1)
            eng.wait_ge(nm.log, 1)
            eng.activation(rstd[:], rstd[:], ACT.Exp, scale=-0.5).then_inc(nm.rstd, 1)

        def gain_col(which, d):
            v = V_NORM + which * DT + d
            return gains[:, v:v + 1]

        def dve_norm(eng, nm, which):
            eng.wait_ge(nm.rstd, 1)
            for d in range(DT + 1):
                if d < DT:
                    if d >= 2:
                        eng.wait_ge(nm.hi, d - 1)
                        eng.wait_ge(nm.lo, d - 1)
                    eng.scalar_tensor_tensor(out=sq_buf[d % 2][:], in0=xT[:, d],
                                             scalar=gain_col(which, d), in1=rstd[:],
                                             op0=ALU.mult, op1=ALU.mult).then_inc(nm.scaled, 1)
                if d:
                    eng.wait_ge(nm.hi, d)
                    eng.tensor_tensor(h_lo[:, d - 1], sq_buf[(d - 1) % 2][:],
                                      h_hi[:, d - 1].bitcast(F32), ALU.subtract).then_inc(nm.lo, 1)

        def act_norm(eng, nm):
            for d in range(DT):
                eng.wait_ge(nm.scaled, d + 1)
                eng.activation(h_hi[:, d], sq_buf[d % 2][:], ACT.Copy).then_inc(nm.hi, 1)

        def sp_ffn(sp, f):
            wgu = w_gate_up[0, f.which]
            wd = w_down[0, f.which]

            def step(g, first=False):
                cols = [wgu[:, bass.ds(addr(sp, g * 2 * P + c0), P)] for c0 in (0, FF, P, FF + P)]
                rows = [wd[bass.ds(addr(sp, g * 2 * P + j * P), P), :] for j in range(2)]
                for j in range(4):
                    load_col(sp, cols[j], f.slot0 + 4 * g + j, j, not (first and f is ffn_a))
                for j in range(2):
                    if not first:
                        sp.wait_ge(f.rlo, 2 * g + j - 1)
                    elif f is ffn_b and j == 0:
                        sp.wait_ge(m_gated, HEADS)
                    sp.dma_start(row_raw[:, j], rows[j]).then_inc(f.rload[j], 16)

            step(0, True)
            with sp.Fori(1, GROUPS) as g:
                step(g)

        def pe_ffn(pe, f):
            def down(m, final=False):
                pe.wait_ge(f.rlo, 2 * m + 2)
                pe.wait_ge(f.alo, 2 * m + 2)
                for d in range(DT):
                    b = (1 + d) % 4
                    if d == 0:
                        pe.wait_ge(f.prod, 2 * m + 1)
                    elif d == 1:
                        pe.wait_ge(f.silu, 2 * m + 2)
                    elif d == 2:
                        pe.wait_ge(f.prod, 2 * m + 2)
                    elif d == 3 and not final:
                        pe.wait_ge(f.silu, 2 * m + 3)
                    elif d == 3:
                        pe.wait_ge(f.xadd, DT * m)
                    else:
                        pe.wait_ge(f.xadd, DT * m + d - 3)
                    for t in range(2):
                        mm = pe_three(pe, bank[b], row_hi[:, t, d * P:(d + 1) * P],
                                      row_lo[:, t, d * P:(d + 1) * P], act_hi[:, t], act_lo[:, t],
                                      t == 0, t == 1)
                    mm.then_inc(f.down, 1)

            def step(g, first=False):
                n = f.slot0 + 4 * g
                if not first:
                    pe.wait_ge(f.silu, 2 * g - 1)
                    pe.wait_ge(f.prod, 2 * g - 1)
                pe_col_unit(pe, n, 0, bank[0], f.norm.lo if first else None)
                if not first:
                    down(g - 1)
                for j in (1, 2, 3):
                    if not first:
                        pe.wait_ge(f.xadd, DT * (g - 1) + 4 + j)
                    pe_col_unit(pe, n + j, j, bank[j])

            step(0, True)
            with pe.Fori(1, GROUPS) as g:
                step(g)
            down(GROUPS - 1, True)

        def act_ffn(act, f, last_phase):
            def silu(g, t):
                act.wait_ge(s_cdone, f.slot0 + 4 * g + 2 * t + 1)
                if not (isinstance(g, int) and g == 0 and t == 0):
                    act.wait_ge(f.prod, 2 * g + t)
                act.activation(silu_g[:], bank[2 * t][:], ACT.Silu).then_inc(f.silu, 1)

            def hidden_hi(g, t):
                act.wait_ge(f.prod, 2 * g + t + 1)
                act.activation(act_hi[:, t], prod[:], ACT.Copy).then_inc(f.ahi, 1)

            def step(g, first=False, last=False):
                n = f.slot0 + 4 * g
                split_hi_col(act, n + 1, 1, not (first and f is ffn_a))
                silu(g, 0)
                split_hi_col(act, n + 2, 2)
                if not first:
                    act.wait_ge(f.down, DT * g)
                for t in range(2):
                    act.wait_ge(f.rload[t], 16 * g + 16)
                    act.activation(row_hi[:, t], row_raw[:, t], ACT.Copy).then_inc(f.rhi, 1)
                hidden_hi(g, 0)
                split_hi_col(act, n + 3, 3)
                silu(g, 1)
                if not last:
                    split_hi_col(act, n + 4, 0)
                hidden_hi(g, 1)

            step(0, True)
            with act.Fori(1, GROUPS - 1) as g:
                step(g)
            step(GROUPS - 1, last=last_phase)

        def pool_ffn(pool, f, last_phase):
            def step(g, last=False):
                n = f.slot0 + 4 * g
                split_lo_col(pool, n + 1, 1)
                split_lo_col(pool, n + 2, 2)
                for t in range(2):
                    pool.wait_ge(f.rhi, 2 * g + t + 1)
                    pool.tensor_tensor(row_lo[:, t], row_raw[:, t], row_hi[:, t].bitcast(F32),
                                       ALU.subtract).then_inc(f.rlo, 1)
                split_lo_col(pool, n + 3, 3)
                if not last:
                    split_lo_col(pool, n + 4, 0)

            with pool.Fori(0, GROUPS - 1) as g:
                step(g)
            step(GROUPS - 1, last_phase)

        def dve_ffn(dve, f, after):
            def down(m, final=False):
                for d in range(DT):
                    dve.wait_ge(f.down, DT * m + d + 1)
                    dve.scalar_tensor_tensor(out=xT[:, d], in0=bank[(1 + d) % 4][:], scalar=0.5,
                                             in1=xT[:, d], op0=ALU.mult, op1=ALU.add).then_inc(f.xadd, 1)
                    if final and d:
                        dve_add_square(dve, after, d - 1)
                if final:
                    dve_add_square(dve, after, DT - 1)

            def step(g, first=False):
                if not first:
                    down(g - 1)
                for t in range(2):
                    if first and t == 0:
                        dve.wait_ge(f.norm.lo, DT)
                    else:
                        dve.wait_ge(f.alo, 2 * g + t)
                    dve.wait_ge(f.silu, 2 * g + t + 1)
                    dve.wait_ge(s_cdone, f.slot0 + 4 * g + 2 * t + 2)
                    dve.tensor_tensor(prod[:], silu_g[:], bank[2 * t + 1][:], ALU.mult).then_inc(f.prod, 1)
                    dve.wait_ge(f.ahi, 2 * g + t + 1)
                    dve.tensor_tensor(act_lo[:, t], prod[:], act_hi[:, t].bitcast(F32),
                                      ALU.subtract).then_inc(f.alo, 1)

            step(0, True)
            with dve.Fori(1, GROUPS) as g:
                step(g)
            down(GROUPS - 1, True)

        small = bank[2]
        LO, UP = slice(0, HALF), slice(HALF, T)
        halves = (LO, UP)

        def blocks(ap, b):
            return ap.rearrange("p (a two b) -> p a two b", two=2, b=b)

        def sp_mixer(sp):
            def step(i):
                cols = [w_in[0][:, bass.ds(addr(sp, i * P + c0), P)] for c0 in (D, 0, 2 * D, 3 * D)]
                for j in range(4):
                    load_col(sp, cols[j], MIX0 + 4 * i + j, j, alone=True)

            step(0)
            sp.wait_ge(ffn_a.xadd, DT * GROUPS)
            sp.dma_start(x_park, xT[:].rearrange("p d t -> p (d t)")).then_inc(s_park, 16)
            with sp.Fori(1, HEADS) as i:
                step(i)

        def pe_mixer(pe):
            def updates(h):
                pe.wait_ge(m_knat, 2 * h + 2)
                pe.wait_ge(m_vnat, 2 * h + 2)
                for c in range(NC - 1):
                    mm = pe.matmul(small[:, c * P:(c + 1) * P], k_nat[:, c], v_nat[:, c],
                                   start=True, stop=True)
                mm.then_inc(m_upd, 1)

            def outputs(h, first=False):
                pe.wait_ge(m_sel, 9 * h + 9)
                pe.wait_ge(m_qcum, h + 1)
                pe.wait_ge(m_state, 7 * h + 7)
                if not first:
                    pe.wait_ge(m_norm, h)
                for c in range(NC):
                    s = slice(c * P, (c + 1) * P)
                    mm = pe.matmul(bank[3][:, s], v_nat[:, c], scores[:, s], start=True, stop=c == 0)
                    if c:
                        mm = pe.matmul(bank[3][:, s], state[:, c], q_cum[:, s], start=False, stop=True)
                mm.then_inc(m_o, 1)

            def head_sum(h):
                pe.wait_ge(m_osq, h + 1)
                for s in halves:
                    mm = pe.matmul(small[:, s], ones[:], logf[:, s], start=True, stop=True)
                mm.then_inc(m_osum, 1)

            def level(i, n, first=False):
                pe.wait_ge(m_ops, 8 * i + n + 1)
                if n >= 2:
                    pe.wait_ge(m_sel, 9 * i + n - 1)
                    if n == 6:
                        pe.wait_ge(m_vnat, 2 * i + 1)
                elif not first:
                    pe.wait_ge(m_hlog, i)
                off = (n % 2) * HALF
                for c in range(NC):
                    keys = k_t if n == NL - 1 else k_dec[:, n % 2]
                    mm = pe.matmul(small[:, off + c * 64:off + (c + 1) * 64],
                                   keys[:, c * P:(c + 1) * P], q_dec[:, n % 2, c * 64:(c + 1) * 64],
                                   start=True, stop=True)
                mm.then_inc(m_lvl, 1)

            def turn(src, half, done):
                for c in range(4):
                    mm = pe.transpose(small[:, half * HALF + c * P:half * HALF + (c + 1) * P],
                                      src[:, half * HALF + c * P:half * HALF + (c + 1) * P], ident[:])
                mm.then_inc(done, 1)

            def diagonal(half, off):
                for c in range(4):
                    s = slice(half * HALF + c * P, half * HALF + (c + 1) * P)
                    mm = pe.matmul(small[:, off + c * P:off + (c + 1) * P], k_t[:, s], q_t[:, s],
                                   start=True, stop=True)
                mm.then_inc(m_lvl, 1)

            def step(i, first=False):
                n = MIX0 + 4 * i
                if not first:
                    pe.wait_ge(m_vt, i)
                pe_col_unit(pe, n, 0, bank[0], norms[1].lo if first else None)
                if not first:
                    updates(i - 1)
                    pe.wait_ge(m_og, i)
                pe_col_unit(pe, n + 1, 1, bank[1])
                if not first:
                    outputs(i - 1)

                def in_v(k):
                    if k == 3 and not first:
                        pe.wait_ge(m_state, 7 * i)
                        head_sum(i - 1)
                    if k == 5:
                        level(i, 0, first)
                    if k == 7:
                        level(i, 1, first)

                pe.wait_ge(m_sigf, i + 1)
                pe_col_unit(pe, n + 2, 2, bank[0], between=in_v)
                pe.wait_ge(m_q, i + 1)
                pe_col_unit(pe, n + 3, 3, bank[1],
                            between=lambda k: level(i, 2 + k // 2) if k % 2 else None)
                pe.wait_ge(m_vt, i + 1)
                pe.wait_ge(m_sel, 9 * i + 5)
                turn(v_t, 0, m_vturn)
                pe.wait_ge(m_sel, 9 * i + 6)
                turn(v_t, 1, m_vturn)
                level(i, 6)
                pe.wait_ge(m_vnat, 2 * i + 2)
                diagonal(0, HALF)
                pe.wait_ge(m_sel, 9 * i + 7)
                diagonal(1, 0)
                pe.wait_ge(m_ops, 8 * i + 8)
                pe.wait_ge(m_sel, 9 * i + 8)
                turn(k_end, 1, m_kturn)
                pe.wait_ge(m_sel, 9 * i + 9)
                turn(k_end, 0, m_kturn)

            step(0, True)
            with pe.Fori(1, HEADS) as i:
                step(i)
            updates(HEADS - 1)
            outputs(HEADS - 1)
            head_sum(HEADS - 1)

        def act_mixer(act):
            def exp(i, n):
                act.wait_ge(m_dif, 8 * i + n + 1)
                s = UP if n == 6 else slice(0, T)
                act.activation(decay[:, n % 2, s], decay[:, n % 2, s], ACT.Exp).then_inc(m_exp, 1)

            def o_square(h):
                act.wait_ge(m_o, h + 1)
                act.activation(logf[:], bank[3][:], ACT.Square).then_inc(m_osq, 1)

            def head_rstd(h):
                act.wait_ge(m_osum, h + 1)
                act.activation(sig_q[:], small[:], ACT.Ln, bias=eps[:], scale=1.0 / HD).then_inc(m_hlog, 1)
                act.wait_ge(m_hlog, h + 1)
                act.activation(sig_q[:], sig_q[:], ACT.Exp, scale=-0.5).then_inc(m_hrstd, 1)

            def step(i, first=False):
                n = MIX0 + 4 * i
                split_hi_col(act, n + 1, 1)
                act.wait_ge(s_cdone, n + 1)
                if not first:
                    act.wait_ge(m_og, i)
                act.activation(sig_a[:], bank[0][:], ACT.Sigmoid).then_inc(m_sigf, 1)
                act.wait_ge(m_sigf, i + 1)
                act.activation(logf[:], sig_a[:], ACT.Ln, bias=lbv[:, L_LB, bass.ds(i, 1)],
                               scale=lbv[:, L_ONE_MINUS, bass.ds(i, 1)]).then_inc(m_logf, 1)
                split_hi_col(act, n + 2, 2)
                act.wait_ge(m_cum, i + 1)
                if not first:
                    act.wait_ge(m_state, 7 * i)
                act.activation(tile_dec[:], cum[:, P - 1:T:P], ACT.Exp).then_inc(m_tdec, 1)
                exp(i, 0)
                exp(i, 1)
                act.wait_ge(s_cdone, n + 2)
                act.activation(sig_q[:], bank[1][:], ACT.Sigmoid).then_inc(m_sigq, 1)
                split_hi_col(act, n + 3, 3)
                if not first:
                    o_square(i - 1)
                exp(i, 2)
                act.activation(q_cum[:], cum[:], ACT.Exp).then_inc(m_qexp, 1)
                if not first:
                    act.wait_ge(m_q, i + 1)
                    head_rstd(i - 1)
                exp(i, 3)
                act.wait_ge(s_cdone, n + 3)
                act.activation(v_t[:], bank[0][:], ACT.Copy).then_inc(m_vt, 1)
                split_hi_col(act, n + 4, 0)
                for m in (4, 5, 6, 7):
                    exp(i, m)
                act.wait_ge(s_cdone, n + 4)
                act.wait_ge(m_k, i + 1)
                act.activation(sig_a[:], bank[1][:], ACT.Sigmoid).then_inc(m_sigg, 1)
                for half in range(2):
                    act.wait_ge(m_vturn, 2 * i + half + 1)
                    act.activation(v_nat[:, 4 * half:4 * half + 4],
                                   small[:, halves[half]].rearrange("p (c v) -> p c v", v=P),
                                   ACT.Copy).then_inc(m_vnat, 1)
                for m, half in enumerate((1, 0)):
                    act.wait_ge(m_kturn, 2 * i + m + 1)
                    act.activation(k_nat[:, 4 * half:4 * half + 4],
                                   small[:, halves[half]].rearrange("p (c v) -> p c v", v=P),
                                   ACT.Copy).then_inc(m_knat, 1)

            step(0, True)
            with act.Fori(1, HEADS) as i:
                step(i)
            split_hi_col(act, OUT0 + 1, 1)
            act.wait_ge(s_cdone, OUT0)
            for h in range(HEADS - 1):
                act.wait_ge(m_gated, h + 1)
                act.activation(h_hi[:, h], og[:, h], ACT.Copy).then_inc(g_hi, 1)
            o_square(HEADS - 1)
            head_rstd(HEADS - 1)
            act.wait_ge(m_gated, HEADS)
            act.activation(h_hi[:, HEADS - 1], og[:, HEADS - 1], ACT.Copy).then_inc(g_hi, 1)

        def pool_mixer(pool):
            def exponents(i, n):
                if n < 2:
                    if not (isinstance(i, int) and i == 0):
                        pool.wait_ge(m_ops, 8 * i + n - 1)
                else:
                    pool.wait_ge(m_ops, 8 * i + n - 1)
                if n == NL:
                    c3 = cum[:].rearrange("p (c t) -> p c t", t=P)
                    pool.tensor_tensor(decay[:, n % 2].rearrange("p (c t) -> p c t", t=P),
                                       c3[:, :, P - 1:P].broadcast_to([P, NC, P]), c3,
                                       ALU.subtract).then_inc(m_dif, 1)
                    return
                b = LEVELS[n]
                c4 = blocks(cum[:], b)
                ref = c4[:, :, 0, b - 1:b].broadcast_to([P, HALF // b, b])
                lo = decay[:, n % 2, LO].rearrange("p (a b) -> p a b", b=b)
                up = decay[:, n % 2, UP].rearrange("p (a b) -> p a b", b=b)
                if b > 1:
                    pool.tensor_tensor(lo, ref, c4[:, :, 0, :], ALU.subtract)
                pool.tensor_tensor(up, c4[:, :, 1, :], ref, ALU.subtract).then_inc(m_dif, 1)

            def step(i):
                n = MIX0 + 4 * i
                split_lo_col(pool, n + 1, 1)
                split_lo_col(pool, n + 2, 2)
                pool.wait_ge(m_cum, i + 1)
                exponents(i, 0)
                exponents(i, 1)
                split_lo_col(pool, n + 3, 3)
                for m in (2, 3, 4):
                    exponents(i, m)
                split_lo_col(pool, n + 4, 0)
                for m in (5, 6, 7):
                    exponents(i, m)

            step(0)
            with pool.Fori(1, HEADS) as i:
                step(i)
            split_lo_col(pool, OUT0 + 1, 1)

        def dve_mixer(dve):
            def state_chain(h):
                dve.wait_ge(m_upd, h + 1)
                dve.wait_ge(m_tdec, h + 1)
                dve.tensor_copy(state[:, 1], small[:, 0:P]).then_inc(m_state, 1)
                for c in range(1, NC - 1):
                    dve.wait_ge(m_state, 7 * h + c)
                    dve.scalar_tensor_tensor(out=state[:, c + 1], in0=state[:, c],
                                             scalar=tile_dec[:, c:c + 1],
                                             in1=small[:, c * P:(c + 1) * P],
                                             op0=ALU.mult, op1=ALU.add).then_inc(m_state, 1)

            def gate(h):
                dve.wait_ge(m_hrstd, h + 1)
                dve.scalar_tensor_tensor(out=sig_q[:], in0=bank[3][:],
                                         scalar=gains[:, V_HEAD:V_HEAD + 1], in1=sig_q[:],
                                         op0=ALU.mult, op1=ALU.mult).then_inc(m_norm, 1)
                dve.wait_ge(m_og, h + 1)
                dve.wait_ge(m_norm, h + 1)
                dve.tensor_tensor(og[:, bass.ds(h, 1)], og[:, bass.ds(h, 1)],
                                  sig_q[:].rearrange("p (o t) -> p o t", o=1),
                                  ALU.mult).then_inc(m_gated, 1)

            def operands(i, n):
                dve.wait_ge(m_exp, 8 * i + n + 1)
                if n == NL:
                    dve.tensor_tensor(k_end[:], k_t[:], decay[:, n % 2], ALU.mult).then_inc(m_ops, 1)
                    return
                if n >= 2:
                    dve.wait_ge(m_lvl, 9 * i + n - 1)
                b = LEVELS[n]
                if b > 1:
                    dve.tensor_tensor(blocks(k_dec[:, n % 2], b)[:, :, 0, :], blocks(k_t[:], b)[:, :, 0, :],
                                      decay[:, n % 2, LO].rearrange("p (a b) -> p a b", b=b), ALU.mult)
                dve.tensor_tensor(q_dec[:, n % 2].rearrange("p (a b) -> p a b", b=b),
                                  blocks(q_t[:], b)[:, :, 1, :],
                                  decay[:, n % 2, UP].rearrange("p (a b) -> p a b", b=b),
                                  ALU.mult).then_inc(m_ops, 1)

            def select(i, n):
                if not (isinstance(i, int) and i == 0 and n == 0):
                    dve.wait_ge(m_sel, 9 * i + n)
                dve.wait_ge(m_lvl, 9 * i + n + 1)
                dve.sem_inc(m_seen, 1)
                if n < NL:
                    b = LEVELS[n]
                    off = (n % 2) * HALF
                    dve.copy_predicated(
                        blocks(scores[:], b)[:, :, 1, :],
                        masks[:, n:n + 1, :].bitcast(U32).rearrange("p o (a b) -> p o a b", b=b)
                        .broadcast_to([P, NC, 64 // b, b]),
                        small[:, off:off + HALF].rearrange("p (c a b) -> p c a b", c=NC, b=b),
                    ).then_inc(m_sel, 1)
                else:
                    half = n - NL
                    off = HALF if half == 0 else 0
                    dve.copy_predicated(
                        scores[:, half * HALF:(half + 1) * HALF].rearrange("p (c t) -> p c t", t=P),
                        ident[:].bitcast(U32).rearrange("p (o t) -> p o t", o=1).broadcast_to([P, 4, P]),
                        small[:, off:off + HALF].rearrange("p (c t) -> p c t", t=P),
                    ).then_inc(m_sel, 1)

            def step(i, first=False):
                n = MIX0 + 4 * i
                if not first:
                    dve.wait_ge(m_kturn, 2 * i)
                dve.wait_ge(m_sigf, i + 1)
                dve.tensor_scalar(k_t[:], sig_a[:], lbv[:, L_MINUS, bass.ds(i, 1)],
                                  lbv[:, L_ONE_MINUS, bass.ds(i, 1)], ALU.mult, ALU.add).then_inc(m_k, 1)
                if not first:
                    state_chain(i - 1)
                dve.wait_ge(m_logf, i + 1)
                for c in range(NC):
                    s = slice(c * P, (c + 1) * P)
                    cs = dve.tensor_tensor_scan(cum[:, s], ones[:], logf[:, s], 0.0, ALU.mult, ALU.add)
                cs.then_inc(m_cum, 1)
                dve.wait_ge(m_sigq, i + 1)
                dve.scalar_tensor_tensor(out=q_t[:], in0=sig_q[:], scalar=QSCALE, in1=bank[1][:],
                                         op0=ALU.mult, op1=ALU.mult).then_inc(m_q, 1)
                dve.wait_ge(m_q, i + 1)
                operands(i, 0)
                operands(i, 1)
                for m in range(2, NL):
                    select(i, m - 2)
                    operands(i, m)
                    if m == 3 and not first:
                        gate(i - 1)
                select(i, NL - 2)
                operands(i, NL)
                dve.wait_ge(m_qexp, i + 1)
                dve.tensor_tensor(q_cum[:], q_cum[:], q_t[:], ALU.mult).then_inc(m_qcum, 1)
                dve.wait_ge(m_sigg, i + 1)
                if first:
                    dve.wait_ge(s_park, 16)
                dve.tensor_tensor(og[:, bass.ds(i, 1)], sig_a[:].rearrange("p (o t) -> p o t", o=1),
                                  bank[1][:].rearrange("p (o t) -> p o t", o=1),
                                  ALU.mult).then_inc(m_og, 1)
                for m in (6, 7, 8):
                    select(i, m)

            dve.memset(scores[:], 0.0).then_inc(m_zero, 1)
            dve.memset(k_dec[:], 0.0).then_inc(m_zero, 1)
            dve.wait_ge(m_zero, 2)
            step(0, True)
            with dve.Fori(1, HEADS) as i:
                step(i)
            state_chain(HEADS - 1)

            def gated_lo(h):
                dve.wait_ge(g_hi, h + 1)
                dve.tensor_tensor(h_lo[:, h], og[:, h], h_hi[:, h].bitcast(F32),
                                  ALU.subtract).then_inc(g_lo, 1)

            for h in range(HEADS - 1):
                gated_lo(h)
            gate(HEADS - 1)
            gated_lo(HEADS - 1)

        @block.sync
        def _(sp):
            sp.dma_start(vec_rows[V_NORM:V_FINAL], norm_gains[0].rearrange("w (a p) -> (w a) p", p=P)).then_inc(s_vec, 16)
            sp.dma_start(vec_rows[V_FINAL:V_LOGIT0], final_gain.rearrange("(a p) -> a p", p=P)).then_inc(s_vec, 16)
            sp.dma_start(vec_rows[V_LOGIT0:V_HEAD], lb_logits.rearrange("w (a p) -> (w a) p", p=P)).then_inc(s_vec, 16)
            sp.dma_start(vec_rows[V_HEAD:NVEC], head_gain).then_inc(s_vec, 16)
            for t in range(NC):
                if t >= 4:
                    sp.wait_ge(s_turned, t - 3)
                sp.dma_start(stage[:, t % 4], x[0, t * P:(t + 1) * P, :]).then_inc(s_xload[t % 4], 16)
            sp_ffn(sp, ffn_a)
            sp_mixer(sp)
            sp.wait_ge(s_park, 16)
            for d in range(4):
                load_col(sp, w_out[0][:, d * P:(d + 1) * P], OUT0 + d, d)
            for d in range(DT):
                sp.wait_ge(g_lo, d + 1)
                sp.dma_start(xT[:, d], x_park[:, d * T:(d + 1) * T]).then_inc(s_back[d], 16)
            for d in range(4, DT):
                load_col(sp, w_out[0][:, d * P:(d + 1) * P], OUT0 + d, d % 4)
            sp_ffn(sp, ffn_b)
            for t in range(NC):
                sp.wait_ge(s_placed_out[t % 2], t // 2 + 1)
                sp.dma_start(out[0, t * P:(t + 1) * P, :], stage[:, t % 4]).then_inc(s_out[t % 4], 16)
            for done in s_out:
                sp.wait_ge(done, 16 * NC // 4)

        @block.gpsimd
        def _(pool):
            pool.memset(ones[:], 1.0).then_inc(s_ones, 1)
            pool.memset(eps[:], EPS).then_inc(s_eps, 1)
            pool.memset(ident[:], 0.0).then_inc(s_ident, 1)
            pool.memset(masks[:], 1.0).then_inc(s_mask, 1)
            pool.wait_ge(s_ident, 1)
            pool.affine_select(out=ident[:], in_=ident[:], compare_op=ALU.not_equal, fill=1.0, base=0,
                               pattern=[[-1, P]], channel_multiplier=1).then_inc(s_ident, 1)
            for n, b in enumerate(LEVELS):
                m = masks[:, n].rearrange("p (a b) -> p a b", b=b)
                pool.wait_ge(s_mask, 2 * n + 1)
                pool.affine_select(out=m, in_=m, compare_op=ALU.is_ge, fill=0.0, base=0,
                                   pattern=[[-2 * b, 64 // b], [0, b]], channel_multiplier=1).then_inc(s_mask, 1)
                pool.wait_ge(s_mask, 2 * n + 2)
                pool.affine_select(out=m, in_=m, compare_op=ALU.is_ge, fill=0.0, base=b - 1,
                                   pattern=[[2 * b, 64 // b], [0, b]], channel_multiplier=-1).then_inc(s_mask, 1)
            split_lo_col(pool, 0, 0)
            pool_ffn(pool, ffn_a, False)
            pool_mixer(pool)
            for m in range(DT // 4):
                n = OUT0 + 4 * m
                for j in (1, 2, 3, 4):
                    if m or j > 1:
                        split_lo_col(pool, n + j, j % 4)
            pool_ffn(pool, ffn_b, True)

        @block.scalar
        def _(act):
            act.wait_ge(s_lb, 3)
            act.activation(lbv[:, L_E0:L_E1 + 1], lbv[:, L_E0:L_E1 + 1], ACT.Exp).then_inc(s_lbexp, 1)
            for t in range(1, NC, 2):
                act.wait_ge(s_turned, t + 1)
                act.activation(xT[:, :, t * P:(t + 1) * P], bank[1][:].rearrange("p (d t) -> p d t", t=P),
                               ACT.Copy).then_inc(s_placed[1], 1)
            act.wait_ge(s_placed[0], NC // 2)
            for d in range(DT):
                act_square(act, norms[0], d, s_placed[1], NC // 2)
            split_hi_col(act, 0, 0, False)
            act.wait_ge(s_eps, 1)
            act_rstd(act, norms[0], bank[3])
            act_norm(act, norms[0])
            act_ffn(act, ffn_a, False)
            for d in range(DT):
                act_square(act, norms[1], d, ffn_a.xadd, DT * (GROUPS - 1) + d + 1)
            act_rstd(act, norms[1], bank[1])
            act_norm(act, norms[1])
            act_mixer(act)
            for m in range(DT // 4):
                n = OUT0 + 4 * m
                for j in (1, 2, 3, 4):
                    if m or j > 1:
                        split_hi_col(act, n + j, j % 4)
                    d = 4 * m + j - 1
                    act_square(act, norms[2], d, o_add, d + 1)
            act_rstd(act, norms[2], bank[0])
            act_norm(act, norms[2])
            act_ffn(act, ffn_b, True)
            for d in range(DT):
                act_square(act, norms[3], d, ffn_b.xadd, DT * (GROUPS - 1) + d + 1)
            act_rstd(act, norms[3], bank[1])
            for t in range(1, NC, 2):
                if t >= 4:
                    act.wait_ge(s_out[t % 4], 16)
                act.wait_ge(s_outturn, t + 1)
                act.activation(stage[:, t % 4], bank[2 + t % 2][:], ACT.Copy).then_inc(s_placed_out[1], 1)

        @block.vector
        def _(dve):
            dve.wait_ge(s_vturn, 1)
            dve.tensor_copy(gains[:], bank[2][:, 0:NVEC]).then_inc(s_gains, 1)
            dve.wait_ge(s_gains, 1)
            l0, l1 = gains[:, V_LOGIT0:V_LOGIT1], gains[:, V_LOGIT1:V_HEAD]
            dve.tensor_tensor(lbv[:, L_MAX], l0, l1, ALU.max).then_inc(s_lb, 1)
            dve.wait_ge(s_lb, 1)
            dve.tensor_tensor(lbv[:, L_E0], l0, lbv[:, L_MAX], ALU.subtract).then_inc(s_lb, 1)
            dve.tensor_tensor(lbv[:, L_E1], l1, lbv[:, L_MAX], ALU.subtract).then_inc(s_lb, 1)
            for t in range(0, NC, 2):
                dve.wait_ge(s_turned, t + 1)
                dve.tensor_copy(xT[:, :, t * P:(t + 1) * P],
                                bank[0][:].rearrange("p (d t) -> p d t", t=P)).then_inc(s_placed[0], 1)
            dve.wait_ge(s_lbexp, 1)
            dve.tensor_tensor(lbv[:, L_SUM], lbv[:, L_E0], lbv[:, L_E1], ALU.add).then_inc(s_lb, 1)
            dve.wait_ge(s_lb, 4)
            dve.reciprocal(lbv[:, L_INV], lbv[:, L_SUM]).then_inc(s_lb, 1)
            dve.wait_ge(s_lb, 5)
            dve.tensor_tensor(lbv[:, L_LB], lbv[:, L_E0], lbv[:, L_INV], ALU.mult).then_inc(s_lb, 1)
            dve.wait_ge(s_lb, 6)
            dve.tensor_scalar(lbv[:, L_ONE_MINUS], lbv[:, L_LB], -1.0, 1.0, ALU.mult, ALU.add).then_inc(s_lb, 1)
            dve.tensor_scalar(lbv[:, L_MINUS], lbv[:, L_LB], 1.0, None, ALU.subtract).then_inc(s_lb, 1)
            dve.wait_ge(s_lb, 8)
            dve.tensor_scalar(lbv[:, L_LB], lbv[:, L_LB], TINY, None, ALU.max).then_inc(s_lb, 1)
            dve.wait_ge(s_lb, 9)
            for d in range(DT):
                dve_add_square(dve, norms[0], d)
            dve_norm(dve, norms[0], 0)
            dve_ffn(dve, ffn_a, norms[1])
            dve_norm(dve, norms[1], 1)
            dve.wait_ge(s_ones, 1)
            dve.wait_ge(s_ident, 2)
            dve.wait_ge(s_mask, 2 * NL + 1)
            dve_mixer(dve)
            for d in range(DT):
                dve.wait_ge(s_cdone, OUT0 + d + 1)
                dve.wait_ge(s_back[d], 16)
                dve.tensor_tensor(xT[:, d], xT[:, d], bank[d % 4][:], ALU.add).then_inc(o_add, 1)
                if d:
                    dve_add_square(dve, norms[2], d - 1)
            dve_add_square(dve, norms[2], DT - 1)
            dve_norm(dve, norms[2], 2)
            dve_ffn(dve, ffn_b, norms[3])
            dve.wait_ge(norms[3].rstd, 1)
            for d in range(DT):
                dve.scalar_tensor_tensor(out=xT[:, d], in0=xT[:, d],
                                         scalar=gains[:, V_FINAL + d:V_FINAL + d + 1], in1=rstd[:],
                                         op0=ALU.mult, op1=ALU.mult).then_inc(norms[3].scaled, 1)
            for t in range(0, NC, 2):
                if t >= 4:
                    dve.wait_ge(s_out[t % 4], 16)
                dve.wait_ge(s_outturn, t + 1)
                dve.tensor_copy(stage[:, t % 4], bank[2 + t % 2][:]).then_inc(s_placed_out[0], 1)

        @block.tensor
        def _(pe):
            pe.wait_ge(s_ident, 2)
            pe.wait_ge(s_vec, 64)
            pe.transpose(bank[2][:, 0:NVEC], vec_rows[:], ident[0:NVEC, 0:NVEC]).then_inc(s_vturn, 1)
            for t in range(NC):
                pe.wait_ge(s_xload[t % 4], 16 * (t // 4 + 1))
                if t >= 2:
                    pe.wait_ge(s_placed[t % 2], t // 2)
                for d in range(DT):
                    mm = pe.transpose(bank[t % 2][:, d * P:(d + 1) * P], stage[:, t % 4, d * P:(d + 1) * P],
                                      ident[:])
                mm.then_inc(s_turned, 1)
            pe.wait_ge(s_ones, 1)
            pe_norm_sum(pe, norms[0], bank[3])
            pe_ffn(pe, ffn_a)
            pe.wait_ge(ffn_a.xadd, DT * GROUPS)
            pe_norm_sum(pe, norms[1], bank[1])
            pe_mixer(pe)
            for d in range(DT):
                if d in (2, 3):
                    pe.wait_ge(m_gated, HEADS)
                if d >= 4:
                    pe.wait_ge(o_add, d - 3)
                pe_col_unit(pe, OUT0 + d, d % 4, bank[d % 4], g_lo if d == 0 else None)
            pe_norm_sum(pe, norms[2], bank[0])
            pe_ffn(pe, ffn_b)
            pe_norm_sum(pe, norms[3], bank[1])
            pe.wait_ge(norms[3].scaled, DT)
            for t in range(NC):
                if t >= 2:
                    pe.wait_ge(s_placed_out[t % 2], t // 2)
                for d in range(DT):
                    mm = pe.transpose(bank[2 + t % 2][:, d * P:(d + 1) * P], xT[:, d, t * P:(t + 1) * P],
                                      ident[:])
                mm.then_inc(s_outturn, 1)


_INS = ['x', 'ffn_w_gate_up', 'ffn_w_down', 'norm_gains', 'final_norm_gain', 'hgrn_w_in',
        'hgrn_lower_bound_logits', 'hgrn_norm_gain', 'hgrn_w_out']


def kernel(**inputs):
    import numpy as np
    import concourse.bacc as bacc
    from concourse.bass_utils import run_bass_kernel_spmd

    nc = bacc.Bacc("TRN2", target_bir_lowering=False, num_devices=1)
    arrays, args = {}, []
    for name in _INS:
        a = np.ascontiguousarray(inputs[name])
        arrays[f"in_{name}"] = a
        args.append(nc.dram_tensor(f"in_{name}", a.shape, mybir.dt.from_np(a.dtype), kind="ExternalInput").ap())
    args.append(nc.dram_tensor("trunk_out", (1, T, D), F32, kind="ExternalOutput").ap())
    hgrn2_trunk(nc, *args)
    r = run_bass_kernel_spmd(nc, [arrays], core_ids=[0])
    return r.results[0]["trunk_out"]
```

```python
from contextlib import ExitStack

import concourse.bass as bass
from concourse import mybir

F32 = mybir.dt.float32
F32R = mybir.dt.float32r
U32 = mybir.dt.uint32
ALU = mybir.AluOpType
ACT = mybir.ActivationFunctionType

P = 128
T = 1024
HALF = 512
LO, UP = slice(0, HALF), slice(HALF, T)
BOTH = (LO, UP)
D = 1024
DT = D // P
FF = 2816
FT = FF // P
GROUPS = FT // 2
HEADS = 8
NC = T // P
LEVELS = (64, 32, 16, 8, 4, 2, 1)
NL = len(LEVELS)
HD = D // HEADS
QSCALE = float(HD) ** -0.5
EPS = 1e-6
V_NORM, V_FINAL, V_LOGIT0, V_LOGIT1, V_HEAD = 0, 3 * DT, 4 * DT, 5 * DT, 6 * DT
NVEC = V_HEAD + 1
L_MAX, L_E0, L_E1, L_SUM, L_INV, L_LB, L_ONE_MINUS, L_MINUS = range(8)
TINY = 2.0 ** -60


def hgrn2_trunk(nc, x, w_gate_up, w_down, norm_gains, final_gain, w_in, lb_logits, head_gain,
                w_out, out):
    ctx = ExitStack()
    with ctx:
        def sb(stack, name, shape, dt=F32):
            return stack.enter_context(nc.sbuf_tensor(name, shape, dt))

        def sem(name):
            return ctx.enter_context(nc.semaphore(name))

        h_hi = sb(ctx, "h_hi", [P, DT, T], F32R)
        h_lo = sb(ctx, "h_lo", [P, DT, T], F32R)
        col_hi = sb(ctx, "col_hi", [P, 2, DT, P], F32R)
        col_lo = sb(ctx, "col_lo", [P, 2, DT, P], F32R)
        col_raw = sb(ctx, "col_raw", [P, 4, DT, P])
        ident = sb(ctx, "ident", [P, P])
        ones = sb(ctx, "ones", [P, P])
        masks = sb(ctx, "masks", [P, NL, P // 2])
        gains = sb(ctx, "gains", [P, NVEC])
        lbv = sb(ctx, "lbv", [P, 8, HEADS])
        vec_rows = sb(ctx, "vec_rows", [NVEC, P])
        eps = sb(ctx, "eps", [P, 1])

        ffn_mem = ExitStack()
        xT = sb(ffn_mem, "xT", [P, DT, T])
        sumsq = sb(ffn_mem, "sumsq", [P, T])
        rstd = sb(ffn_mem, "rstd", [P, T])
        act_hi = sb(ffn_mem, "act_hi", [P, 2, T], F32R)
        act_lo = sb(ffn_mem, "act_lo", [P, 2, T], F32R)
        row_hi = sb(ffn_mem, "row_hi", [P, 2, D], F32R)
        row_lo = sb(ffn_mem, "row_lo", [P, 2, D], F32R)
        row_raw = sb(ffn_mem, "row_raw", [P, 2, D])
        silu_g = sb(ffn_mem, "silu_g", [P, T])
        prod = sb(ffn_mem, "prod", [P, T])
        stage = sb(ffn_mem, "stage", [P, 4, D])
        ffn_mem.close()

        mix_mem = ExitStack()
        og = sb(mix_mem, "og", [P, HEADS, T])
        sig_a = sb(mix_mem, "sig_a", [P, T])
        sig_q = sb(mix_mem, "sig_q", [P, T])
        logf = sb(mix_mem, "logf", [P, T])
        cum = sb(mix_mem, "cum", [P, T])
        k_t = sb(mix_mem, "k_t", [P, T])
        q_t = sb(mix_mem, "q_t", [P, T])
        decay = sb(mix_mem, "decay", [P, 2, T])
        k_dec = sb(mix_mem, "k_dec", [P, 2, T])
        q_dec = sb(mix_mem, "q_dec", [P, 2, HALF])
        q_cum = sb(mix_mem, "q_cum", [P, T])
        k_end = sb(mix_mem, "k_end", [P, T])
        k_nat = sb(mix_mem, "k_nat", [P, NC, P])
        v_t = sb(mix_mem, "v_t", [P, T])
        v_nat = sb(mix_mem, "v_nat", [P, NC, P])
        scores = sb(mix_mem, "scores", [P, T])
        state = sb(mix_mem, "state", [P, NC, P])
        tile_dec = sb(mix_mem, "tile_dec", [P, NC])
        mix_mem.close()

        bank = [ctx.enter_context(nc.psum_tensor(f"bank{i}", [P, T], F32)) for i in range(4)]

        x_park = nc.dram_tensor("x_park", (P, DT * T), F32, kind="Internal").ap()

        block = ctx.enter_context(nc.Block())

        s_xload = [sem(f"x_rows_loaded{i}") for i in range(4)]
        s_vec = sem("vectors_loaded")
        s_ident = sem("identity_steps")
        s_ones = sem("ones_made")
        s_mask = sem("mask_steps")
        s_eps = sem("eps_made")
        s_turned = sem("x_tiles_turned")
        s_placed = [sem("x_placed_by_vector"), sem("x_placed_by_scalar")]
        s_vturn = sem("vectors_turned")
        s_gains = sem("gains_placed")
        s_lb = sem("lower_bound_steps")
        s_lbexp = sem("lower_bound_exps")
        s_cload = [sem(f"col_loaded{i}") for i in range(4)]
        s_chi = sem("col_hi_made")
        s_clo = sem("col_lo_made")
        s_cdone = sem("col_units_done")
        s_park = sem("x_parked")
        s_back = [sem(f"x_back{d}") for d in range(DT)]
        s_gained = sem("x_times_gain")
        s_final = [sem("x_scaled_by_vector"), sem("x_scaled_by_gpsimd")]
        s_outturn = sem("out_tiles_turned")
        s_placed_out = [sem("out_rows_by_vector"), sem("out_rows_by_scalar")]
        s_out = [sem(f"rows_written{i}") for i in range(4)]

        class Norm:

            def __init__(self, tag):
                self.squared = sem(f"{tag}_squared")
                self.added = sem(f"{tag}_added")
                self.summed = sem(f"{tag}_summed")
                self.log = sem(f"{tag}_log")
                self.rstd = sem(f"{tag}_rstd")
                self.scaled = sem(f"{tag}_scaled")
                self.hi = sem(f"{tag}_hi")
                self.lo = [sem(f"{tag}_lo_even"), sem(f"{tag}_lo_odd")]

        class Ffn:
            def __init__(self, tag, which, slot0, norm, after, first_split):
                self.which, self.slot0 = which, slot0
                self.first_split = first_split
                self.norm, self.after = norm, after
                self.rload = [sem(f"{tag}_row_loaded{i}") for i in range(2)]
                self.rhi = sem(f"{tag}_row_hi_made")
                self.rlo = sem(f"{tag}_row_lo_made")
                self.silu = sem(f"{tag}_silu_made")
                self.prod = sem(f"{tag}_prod_made")
                self.ahi = sem(f"{tag}_act_hi_made")
                self.alo = sem(f"{tag}_act_lo_made")
                self.down = sem(f"{tag}_down_done")
                self.xadd = sem(f"{tag}_x_added")
                self.last_up = sem(f"{tag}_last_up_first_half")
                self.last_prod = sem(f"{tag}_last_prod_halves")
                self.last_ahi = sem(f"{tag}_last_act_hi_halves")
                self.last_alo = sem(f"{tag}_last_act_lo_halves")

        norms = [Norm(f"norm{i}") for i in range(4)]
        MIX0 = 4 * GROUPS
        OUT0 = MIX0 + 4 * HEADS
        FFN0 = OUT0 + DT
        SLOTS = FFN0 + 4 * GROUPS
        ffn_a = Ffn("ffn_a", 0, 0, norms[0], norms[1], (col_hi, col_lo))
        ffn_b = Ffn("ffn_b", 1, FFN0, norms[2], norms[3],
                    [row[:].rearrange("p t (k c) -> p t k c", c=P) for row in (row_hi, row_lo)])

        m_sigf = sem("m_sigmoid_f")
        m_logf = sem("m_log_f")
        m_k = sem("m_k_made")
        m_cum = sem("m_cum_made")
        m_tdec = sem("m_tile_decay")
        m_sigq = sem("m_sigmoid_q")
        m_q = sem("m_q_made")
        m_vt = sem("m_v_copied")
        m_sigg = sem("m_sigmoid_g")
        m_og = sem("m_out_gate")
        m_dif = sem("m_exponent_made")
        m_exp = sem("m_decay_made")
        m_ops = sem("m_decayed_operands")
        m_lvl = sem("m_level_scored")
        m_sel = sem("m_level_selected")
        m_vturn = sem("m_v_turned")
        m_vnat = sem("m_v_rows")
        m_kturn = sem("m_k_turned")
        m_knat = sem("m_k_rows")
        m_qexp = sem("m_exp_cum")
        m_qcum = sem("m_q_cum")
        m_upd = sem("m_state_products")
        m_state = sem("m_state_steps")
        m_o = sem("m_o_done")
        m_osq = sem("m_o_squared")
        m_osum = sem("m_o_summed")
        m_hlog = sem("m_head_log")
        m_hrstd = sem("m_head_rstd")
        m_norm = sem("m_o_normed")
        m_gated = sem("m_gated")
        m_zero = sem("m_buffers_zeroed")
        m_seen = sem("m_level_wait_passed")
        s_seen = sem("load_wait_passed")
        g_hi = sem("gated_hi_made")
        g_lo = sem("gated_lo_made")
        o_last = sem("mixer_last_units_first_half")
        o_add = sem("mixer_x_added")

        def addr(eng, value):
            return value if isinstance(value, int) else eng.snap(value)

        def load_col(eng, src, n, r, started=True, alone=False):
            if started:
                eng.wait_ge(s_clo, n - 3)
            if alone:
                eng.sem_inc(s_seen, 1)
            eng.dma_start(col_raw[:, r], src.rearrange("(k p) c -> p k c", p=P)).then_inc(s_cload[r], 16)

        def split_hi_col(eng, n, r, started=True, hi=col_hi):
            eng.wait_ge(s_cload[r], (n - r) * 4 + 16)
            if started:
                eng.wait_ge(s_cdone, n - 1)
            eng.activation(hi[:, r % 2], col_raw[:, r], ACT.Copy).then_inc(s_chi, 1)

        def split_lo_col(eng, n, r, hi=col_hi, lo=col_lo):
            eng.wait_ge(s_chi, n + 1)
            eng.tensor_tensor(lo[:, r % 2], col_raw[:, r], hi[:, r % 2].bitcast(F32),
                              ALU.subtract).then_inc(s_clo, 1)

        def pe_three(eng, dst, w_hi, w_lo, a_hi, a_lo, first, last, over=BOTH):
            for n, a in enumerate((a_hi, a_lo)):
                for s in over:
                    eng.matmul(dst[:, s], w_hi, a[:, s], start=first and n == 0, stop=False)
            for s in over:
                mm = eng.matmul(dst[:, s], w_lo, a_hi[:, s], start=False, stop=last)
            return mm

        def pe_col_tile(eng, r, k, dst, over=BOTH, split=(col_hi, col_lo)):
            return pe_three(eng, dst, split[0][:, r % 2, k], split[1][:, r % 2, k], h_hi[:, k], h_lo[:, k],
                            k == 0, k == DT - 1, over)

        def pe_col_unit(eng, n, r, dst, between=None):
            eng.wait_ge(s_clo, n + 1)
            for k in range(DT):
                mm = pe_col_tile(eng, r, k, dst)
                if k == DT - 1:
                    mm.then_inc(s_cdone, 1)
                if between:
                    between(k)

        def pe_first_units(eng, n, nm, split=(col_hi, col_lo), sum_after=3):
            for c, s in enumerate(BOTH):
                for k in range(DT):
                    eng.wait_ge(nm.lo[k % 2], 4 * c + k // 2 + 1)
                    for u in range(2):
                        if c == 0 and k == 0:
                            eng.wait_ge(s_clo, n + u + 1)
                        mm = pe_col_tile(eng, u, k, bank[u], (s,), split)
                        if c == 1 and k == DT - 1:
                            mm.then_inc(s_cdone, 1)
                    if c == 0 and k == sum_after:
                        pe_norm_sum(eng, nm, 1, bank[2])

        sq_buf = (silu_g, prod)

        def act_square(eng, nm, c, d, ready=None, count=None):
            if ready is not None:
                eng.wait_ge(ready, count)
            q = DT * c + d
            if d >= 2:
                eng.wait_ge(nm.added, q - 1)
            eng.activation(sq_buf[d % 2][:, BOTH[c]], xT[:, d, BOTH[c]], ACT.Square).then_inc(nm.squared, 1)

        def dve_add_square(eng, nm, c, d):
            q = DT * c + d
            s = BOTH[c]
            eng.wait_ge(nm.squared, q + 1)
            if d:
                eng.wait_ge(nm.added, q)
                eng.tensor_tensor(sumsq[:, s], sumsq[:, s], sq_buf[d % 2][:, s], ALU.add).then_inc(nm.added, 1)
            else:
                eng.tensor_copy(sumsq[:, s], sq_buf[0][:, s]).then_inc(nm.added, 1)

        def pe_norm_sum(eng, nm, c, dst):
            eng.wait_ge(nm.added, DT * (c + 1))
            eng.matmul(dst[:, BOTH[c]], ones[:], sumsq[:, BOTH[c]], start=True, stop=True).then_inc(nm.summed, 1)

        def act_rstd(eng, nm, c, src):
            s = BOTH[c]
            eng.wait_ge(nm.summed, c + 1)
            eng.activation(rstd[:, s], src[:, s], ACT.Ln, bias=eps[:], scale=1.0 / D).then_inc(nm.log, 1)
            eng.wait_ge(nm.log, c + 1)
            eng.activation(rstd[:, s], rstd[:, s], ACT.Exp, scale=-0.5).then_inc(nm.rstd, 1)

        def gain_col(which, d):
            v = V_NORM + which * DT + d
            return gains[:, v:v + 1]

        def dve_scale(eng, nm, which, c, d):
            s = BOTH[c]
            if d == 0:
                eng.wait_ge(nm.rstd, c + 1)
            if d >= 2:
                eng.wait_ge(nm.hi, DT * c + d - 1)
                eng.wait_ge(nm.lo[d % 2], 4 * c + d // 2)
            eng.scalar_tensor_tensor(out=sq_buf[d % 2][:, s], in0=xT[:, d, s], scalar=gain_col(which, d),
                                     in1=rstd[:, s], op0=ALU.mult, op1=ALU.mult).then_inc(nm.scaled, 1)

        def act_h_hi(eng, nm, c, d):
            eng.wait_ge(nm.scaled, DT * c + d + 1)
            eng.activation(h_hi[:, d, BOTH[c]], sq_buf[d % 2][:, BOTH[c]], ACT.Copy).then_inc(nm.hi, 1)

        def h_lo_part(eng, nm, c, d):
            s = BOTH[c]
            eng.wait_ge(nm.hi, DT * c + d + 1)
            eng.tensor_tensor(h_lo[:, d, s], sq_buf[d % 2][:, s], h_hi[:, d, s].bitcast(F32),
                              ALU.subtract).then_inc(nm.lo[d % 2], 1)

        def dve_h_tile(eng, nm, which, c, d):
            dve_scale(eng, nm, which, c, d)
            if d % 2:
                h_lo_part(eng, nm, c, d - 1)

        def pool_norm(eng, nm):
            for c in range(2):
                for d in range(1, DT, 2):
                    h_lo_part(eng, nm, c, d)

        def sp_ffn(sp, f):
            wgu = w_gate_up[0, f.which]
            wd = w_down[0, f.which]

            def step(g, first=False):
                cols = [wgu[:, bass.ds(addr(sp, g * 2 * P + c0), P)] for c0 in (0, FF, P, FF + P)]
                rows = [wd[bass.ds(addr(sp, g * 2 * P + j * P), P), :] for j in range(2)]
                for j in range(4):
                    load_col(sp, cols[j], f.slot0 + 4 * g + j, j, not (first and f is ffn_a))
                for j in range(2):
                    if not first:
                        sp.wait_ge(f.rlo, 2 * g + j - 1)
                    elif f is ffn_b and j == 0:
                        sp.wait_ge(m_gated, HEADS)
                    sp.dma_start(row_raw[:, j], rows[j]).then_inc(f.rload[j], 16)

            step(0, True)
            with sp.Fori(1, GROUPS) as g:
                step(g)

        def pe_ffn(pe, f):
            def down(m):
                pe.wait_ge(f.rlo, 2 * m + 2)
                pe.wait_ge(f.alo, 2 * m + 2)
                for d in range(DT):
                    b = (1 + d) % 4
                    if d == 0:
                        pe.wait_ge(f.prod, 2 * m + 1)
                    elif d == 1:
                        pe.wait_ge(f.silu, 2 * m + 2)
                    elif d == 2:
                        pe.wait_ge(f.prod, 2 * m + 2)
                    elif d == 3:
                        pe.wait_ge(f.silu, 2 * m + 3)
                    else:
                        pe.wait_ge(f.xadd, DT * m + d - 3)
                    for t in range(2):
                        mm = pe_three(pe, bank[b], row_hi[:, t, d * P:(d + 1) * P],
                                      row_lo[:, t, d * P:(d + 1) * P], act_hi[:, t], act_lo[:, t],
                                      t == 0, t == 1)
                    mm.then_inc(f.down, 1)

            def last_down():
                m = GROUPS - 1
                pe.wait_ge(f.rlo, 2 * m + 2)
                pe.wait_ge(f.alo, 2 * m + 1)
                pe.wait_ge(f.silu, 2 * m + 2)
                for c in range(2):
                    pe.wait_ge(f.last_alo, c + 1)
                    for d in range(DT):
                        q = DT * c + d
                        if q >= 4:
                            pe.wait_ge(f.xadd, DT * m + q - 3)
                        if (c, d) == (1, 3):
                            pe_norm_sum(pe, f.after, 0, bank[1])
                        for t in range(2):
                            mm = pe_three(pe, bank[(1 + d) % 4], row_hi[:, t, d * P:(d + 1) * P],
                                          row_lo[:, t, d * P:(d + 1) * P], act_hi[:, t], act_lo[:, t],
                                          t == 0, t == 1, (BOTH[c],))
                        mm.then_inc(f.down, 1)

            def step(g, last=False):
                n = f.slot0 + 4 * g
                pe.wait_ge(f.silu, 2 * g - 1)
                pe.wait_ge(f.prod, 2 * g - 1)
                pe_col_unit(pe, n, 0, bank[0])
                down(g - 1)
                for j in (1, 2, 3):
                    pe.wait_ge(f.xadd, DT * (g - 1) + 4 + j)
                    if not last or j < 3:
                        pe_col_unit(pe, n + j, j, bank[j])
                if last:
                    pe.wait_ge(s_clo, n + 4)
                    for c in range(2):
                        for k in range(DT):
                            mm = pe_col_tile(pe, 3, k, bank[3], (BOTH[c],))
                        mm.then_inc(s_cdone if c else f.last_up, 1)

            pe_first_units(pe, f.slot0, f.norm, f.first_split, DT - 1 if f is ffn_a else 3)
            for j in (2, 3):
                pe_col_unit(pe, f.slot0 + j, j, bank[j])
            with pe.Fori(1, GROUPS - 1) as g:
                step(g)
            step(GROUPS - 1, last=True)
            last_down()

        def act_ffn(act, f):
            def silu(g, t):
                act.wait_ge(s_cdone, f.slot0 + 4 * g + 2 * t + 1)
                if not (isinstance(g, int) and g == 0 and t == 0):
                    act.wait_ge(f.prod, 2 * g + t)
                act.activation(silu_g[:], bank[2 * t][:], ACT.Silu).then_inc(f.silu, 1)

            def hidden_hi(g, t):
                act.wait_ge(f.prod, 2 * g + t + 1)
                act.activation(act_hi[:, t], prod[:], ACT.Copy).then_inc(f.ahi, 1)

            def step(g, first=False, last=False):
                n = f.slot0 + 4 * g
                if not first:
                    split_hi_col(act, n + 1, 1)
                silu(g, 0)
                split_hi_col(act, n + 2, 2)
                if first:
                    act.wait_ge(s_cdone, f.slot0 + 2)
                else:
                    act.wait_ge(f.down, DT * g)
                for t in range(2):
                    act.wait_ge(f.rload[t], 16 * g + 16)
                    act.activation(row_hi[:, t], row_raw[:, t], ACT.Copy).then_inc(f.rhi, 1)
                hidden_hi(g, 0)
                split_hi_col(act, n + 3, 3)
                silu(g, 1)
                if not last:
                    split_hi_col(act, n + 4, 0)
                    hidden_hi(g, 1)
                else:
                    for c, s in enumerate(BOTH):
                        act.wait_ge(f.last_prod, c + 1)
                        act.activation(act_hi[:, 1, s], prod[:, s], ACT.Copy).then_inc(f.last_ahi, 1)

            step(0, True)
            with act.Fori(1, GROUPS - 1) as g:
                step(g)
            step(GROUPS - 1, last=True)

        DVE_SCALES = (4, 5)

        def act_norm_after(act, nm, ready, base, slot):
            hi = slot is not None
            if hi:
                split_hi_col(act, slot, 0)
            for d in range(DT):
                act_square(act, nm, 0, d, ready, base + d + 1)
                if hi and d == 2:
                    split_hi_col(act, slot + 1, 1)
            for d in range(DT):
                act_square(act, nm, 1, d, ready, base + DT + d + 1)
                if d == 3:
                    act_rstd(act, nm, 0, bank[1])
                if hi and d >= 4:
                    act_h_hi(act, nm, 0, d - 4)
                elif not hi and 2 <= d < 2 + DT - DVE_SCALES[0]:
                    act_gain(act, 0, DVE_SCALES[0] + d - 2)
            if not hi:
                for d in range(DVE_SCALES[1], DT):
                    act_gain(act, 1, d)
            if hi:
                for d in range(4, DT):
                    act_h_hi(act, nm, 0, d)
            act_rstd(act, nm, 1, bank[2])
            if hi:
                for d in range(DT):
                    act_h_hi(act, nm, 1, d)

        def pool_ffn(pool, f):
            def step(g, first=False, last=False):
                n = f.slot0 + 4 * g
                if not first:
                    split_lo_col(pool, n + 1, 1)
                split_lo_col(pool, n + 2, 2)
                for t in range(2):
                    pool.wait_ge(f.rhi, 2 * g + t + 1)
                    pool.tensor_tensor(row_lo[:, t], row_raw[:, t], row_hi[:, t].bitcast(F32),
                                       ALU.subtract).then_inc(f.rlo, 1)
                split_lo_col(pool, n + 3, 3)
                if not last:
                    split_lo_col(pool, n + 4, 0)

            step(0, True)
            with pool.Fori(1, GROUPS - 1) as g:
                step(g)
            step(GROUPS - 1, last=True)

        def dve_ffn(dve, f, scale):
            def down(m):
                for d in range(DT):
                    dve.wait_ge(f.down, DT * m + d + 1)
                    dve.scalar_tensor_tensor(out=xT[:, d], in0=bank[(1 + d) % 4][:], scalar=0.5,
                                             in1=xT[:, d], op0=ALU.mult, op1=ALU.add).then_inc(f.xadd, 1)

            def last_down():
                for c in range(2):
                    s = BOTH[c]
                    for d in range(DT):
                        dve.wait_ge(f.down, DT * (GROUPS - 1) + DT * c + d + 1)
                        dve.scalar_tensor_tensor(out=xT[:, d, s], in0=bank[(1 + d) % 4][:, s], scalar=0.5,
                                                 in1=xT[:, d, s], op0=ALU.mult, op1=ALU.add).then_inc(f.xadd, 1)
                        if d:
                            dve_add_square(dve, f.after, c, d - 1)
                        if c == 1 and d >= 4:
                            scale(0, d - 4)
                    dve_add_square(dve, f.after, c, DT - 1)
                for d in range(4, DT):
                    scale(0, d)
                for d in range(DT):
                    scale(1, d)

            def step(g, first=False, last=False):
                if not first:
                    down(g - 1)
                for t in range(1 if last else 2):
                    if first and t == 0:
                        dve.wait_ge(f.norm.lo[1], DT)
                    else:
                        dve.wait_ge(f.alo, 2 * g + t)
                    dve.wait_ge(f.silu, 2 * g + t + 1)
                    dve.wait_ge(s_cdone, f.slot0 + 4 * g + 2 * t + 2)
                    dve.tensor_tensor(prod[:], silu_g[:], bank[2 * t + 1][:], ALU.mult).then_inc(f.prod, 1)
                    dve.wait_ge(f.ahi, 2 * g + t + 1)
                    dve.tensor_tensor(act_lo[:, t], prod[:], act_hi[:, t].bitcast(F32),
                                      ALU.subtract).then_inc(f.alo, 1)

            def last_hidden():
                dve.wait_ge(f.alo, 2 * GROUPS - 1)
                dve.wait_ge(f.silu, 2 * GROUPS)
                for c, s in enumerate(BOTH):
                    if c == 0:
                        dve.wait_ge(f.last_up, 1)
                    else:
                        dve.wait_ge(s_cdone, f.slot0 + 4 * GROUPS)
                    dve.tensor_tensor(prod[:, s], silu_g[:, s], bank[3][:, s], ALU.mult).then_inc(f.last_prod, 1)
                    dve.wait_ge(f.last_ahi, c + 1)
                    dve.tensor_tensor(act_lo[:, 1, s], prod[:, s], act_hi[:, 1, s].bitcast(F32),
                                      ALU.subtract).then_inc(f.last_alo, 1)

            step(0, True)
            with dve.Fori(1, GROUPS - 1) as g:
                step(g)
            step(GROUPS - 1, last=True)
            last_hidden()
            last_down()

        small = bank[2]

        def blocks(ap, b):
            return ap.rearrange("p (a two b) -> p a two b", two=2, b=b)

        def sp_mixer(sp):
            def step(i):
                cols = [w_in[0][:, bass.ds(addr(sp, i * P + c0), P)] for c0 in (D, 0, 2 * D, 3 * D)]
                for j in range(4):
                    load_col(sp, cols[j], MIX0 + 4 * i + j, j, alone=True)

            step(0)
            sp.wait_ge(ffn_a.xadd, DT * (GROUPS + 1))
            sp.dma_start(x_park, xT[:].rearrange("p d t -> p (d t)")).then_inc(s_park, 16)
            with sp.Fori(1, HEADS) as i:
                step(i)

        def pe_mixer(pe):
            def updates(h):
                pe.wait_ge(m_knat, 2 * h + 2)
                pe.wait_ge(m_vnat, 2 * h + 2)
                pe.wait_ge(m_sel, 9 * h + 9)
                for c in range(NC - 1):
                    mm = pe.matmul(small[:, c * P:(c + 1) * P], k_nat[:, c], v_nat[:, c],
                                   start=True, stop=True)
                mm.then_inc(m_upd, 1)

            def outputs(h, first=False):
                pe.wait_ge(m_qcum, h + 1)
                pe.wait_ge(m_state, 7 * h + 7)
                if not first:
                    pe.wait_ge(m_norm, h)
                for c in range(NC):
                    s = slice(c * P, (c + 1) * P)
                    mm = pe.matmul(bank[3][:, s], v_nat[:, c], scores[:, s], start=True, stop=c == 0)
                    if c:
                        mm = pe.matmul(bank[3][:, s], state[:, c], q_cum[:, s], start=False, stop=True)
                mm.then_inc(m_o, 1)

            def head_sum(h):
                pe.wait_ge(m_osq, h + 1)
                for s in BOTH:
                    mm = pe.matmul(small[:, s], ones[:], logf[:, s], start=True, stop=True)
                mm.then_inc(m_osum, 1)

            def level(i, n, first=False):
                pe.wait_ge(m_ops, 8 * i + n + 1)
                if n >= 2:
                    pe.wait_ge(m_sel, 9 * i + n - 1)
                elif not first:
                    pe.wait_ge(m_hlog, i)
                off = (n % 2) * HALF
                for c in range(NC):
                    keys = k_t if n == NL - 1 else k_dec[:, n % 2]
                    mm = pe.matmul(small[:, off + c * 64:off + (c + 1) * 64],
                                   keys[:, c * P:(c + 1) * P], q_dec[:, n % 2, c * 64:(c + 1) * 64],
                                   start=True, stop=True)
                mm.then_inc(m_lvl, 1)

            def turn(src, half, place, done):
                for c in range(4):
                    mm = pe.transpose(place[:, c * P:(c + 1) * P],
                                      src[:, half * HALF + c * P:half * HALF + (c + 1) * P], ident[:])
                mm.then_inc(done, 1)

            def diagonal(half, place):
                for c in range(4):
                    s = slice(half * HALF + c * P, half * HALF + (c + 1) * P)
                    mm = pe.matmul(place[:, c * P:(c + 1) * P], k_t[:, s], q_t[:, s], start=True, stop=True)
                mm.then_inc(m_lvl, 1)

            def step(i, first=False):
                n = MIX0 + 4 * i
                if first:
                    pe_first_units(pe, n, norms[1])
                else:
                    pe.wait_ge(m_vt, i)
                    pe_col_unit(pe, n, 0, bank[0])
                    updates(i - 1)
                    pe.wait_ge(m_og, i)
                    pe_col_unit(pe, n + 1, 1, bank[1])
                    outputs(i - 1)

                def in_v(k):
                    if k == 3 and not first:
                        head_sum(i - 1)
                    if k == 5:
                        level(i, 0, first)
                    if k == 7:
                        level(i, 1, first)

                pe.wait_ge(m_sigf, i + 1)
                pe_col_unit(pe, n + 2, 2, bank[0], between=in_v)
                pe.wait_ge(m_q, i + 1)
                pe_col_unit(pe, n + 3, 3, bank[1],
                            between=lambda k: level(i, 2 + k // 2) if k % 2 else None)
                pe.wait_ge(m_vt, i + 1)
                if not first:
                    pe.wait_ge(m_norm, i)
                turn(v_t, 0, bank[3][:, LO], m_vturn)
                turn(v_t, 1, bank[3][:, UP], m_vturn)
                level(i, 6)
                pe.wait_ge(m_sel, 9 * i + 6)
                diagonal(0, small[:, UP])
                pe.wait_ge(m_vnat, 2 * i + 1)
                diagonal(1, bank[3][:, LO])
                pe.wait_ge(m_ops, 8 * i + 8)
                pe.wait_ge(m_vnat, 2 * i + 2)
                turn(k_end, 1, bank[3][:, UP], m_kturn)
                pe.wait_ge(m_sel, 9 * i + 7)
                turn(k_end, 0, small[:, LO], m_kturn)

            step(0, True)
            with pe.Fori(1, HEADS) as i:
                step(i)

            def out_tiles(u, heads):
                for k in heads:
                    if u == 0:
                        pe.wait_ge(g_lo, k + 1)
                    mm = pe_col_tile(pe, u, k, bank[u])
                if k == DT - 1:
                    mm.then_inc(s_cdone, 1)

            updates(HEADS - 1)
            pe.wait_ge(s_clo, OUT0 + 1)
            pe.wait_ge(m_og, HEADS)
            out_tiles(0, range(0, 3))
            outputs(HEADS - 1)
            out_tiles(0, range(3, 5))
            head_sum(HEADS - 1)
            out_tiles(0, range(5, DT - 1))
            pe.wait_ge(s_clo, OUT0 + 2)
            out_tiles(1, range(0, DT - 2))
            out_tiles(0, (DT - 1,))
            out_tiles(1, (DT - 2, DT - 1))

        def act_mixer(act):
            def exp(i, n):
                act.wait_ge(m_dif, 8 * i + n + 1)
                s = UP if n == 6 else slice(0, T)
                act.activation(decay[:, n % 2, s], decay[:, n % 2, s], ACT.Exp).then_inc(m_exp, 1)

            def o_square(h):
                act.wait_ge(m_o, h + 1)
                act.activation(logf[:], bank[3][:], ACT.Square).then_inc(m_osq, 1)

            def head_rstd(h):
                act.wait_ge(m_osum, h + 1)
                act.activation(sig_q[:], small[:], ACT.Ln, bias=eps[:], scale=1.0 / HD).then_inc(m_hlog, 1)
                act.wait_ge(m_hlog, h + 1)
                act.activation(sig_q[:], sig_q[:], ACT.Exp, scale=-0.5).then_inc(m_hrstd, 1)

            def step(i, first=False):
                n = MIX0 + 4 * i
                if not first:
                    split_hi_col(act, n + 1, 1)
                act.wait_ge(s_cdone, n + 1)
                if not first:
                    act.wait_ge(m_og, i)
                act.activation(sig_a[:], bank[0][:], ACT.Sigmoid).then_inc(m_sigf, 1)
                act.wait_ge(m_sigf, i + 1)
                act.activation(logf[:], sig_a[:], ACT.Ln, bias=lbv[:, L_LB, bass.ds(i, 1)],
                               scale=lbv[:, L_ONE_MINUS, bass.ds(i, 1)]).then_inc(m_logf, 1)
                split_hi_col(act, n + 2, 2)
                act.wait_ge(m_cum, i + 1)
                if not first:
                    act.wait_ge(m_state, 7 * i)
                act.activation(tile_dec[:], cum[:, P - 1:T:P], ACT.Exp).then_inc(m_tdec, 1)
                exp(i, 0)
                exp(i, 1)
                act.wait_ge(s_cdone, n + 2)
                act.activation(sig_q[:], bank[1][:], ACT.Sigmoid).then_inc(m_sigq, 1)
                split_hi_col(act, n + 3, 3)
                if not first:
                    o_square(i - 1)
                exp(i, 2)
                act.activation(q_cum[:], cum[:], ACT.Exp).then_inc(m_qexp, 1)
                if not first:
                    act.wait_ge(m_q, i + 1)
                    head_rstd(i - 1)
                exp(i, 3)
                act.wait_ge(s_cdone, n + 3)
                act.activation(v_t[:], bank[0][:], ACT.Copy).then_inc(m_vt, 1)
                split_hi_col(act, n + 4, 0)
                for m in (4, 5, 6, 7):
                    exp(i, m)
                act.wait_ge(s_cdone, n + 4)
                act.wait_ge(m_k, i + 1)
                act.activation(sig_a[:], bank[1][:], ACT.Sigmoid).then_inc(m_sigg, 1)
                for half in range(2):
                    act.wait_ge(m_vturn, 2 * i + half + 1)
                    act.activation(v_nat[:, 4 * half:4 * half + 4],
                                   bank[3][:, BOTH[half]].rearrange("p (c v) -> p c v", v=P),
                                   ACT.Copy).then_inc(m_vnat, 1)
                for m, (half, place) in enumerate(((1, bank[3]), (0, small))):
                    act.wait_ge(m_kturn, 2 * i + m + 1)
                    act.activation(k_nat[:, 4 * half:4 * half + 4],
                                   place[:, BOTH[half]].rearrange("p (c v) -> p c v", v=P),
                                   ACT.Copy).then_inc(m_knat, 1)

            step(0, True)
            with act.Fori(1, HEADS) as i:
                step(i)
            act.wait_ge(s_cdone, OUT0)
            for h in range(HEADS - 1):
                if h == 2:
                    split_hi_col(act, OUT0 + 1, 1)
                act.wait_ge(m_gated, h + 1)
                act.activation(h_hi[:, h], og[:, h], ACT.Copy).then_inc(g_hi, 1)
                if h == 4:
                    o_square(HEADS - 1)
            head_rstd(HEADS - 1)
            act.wait_ge(m_gated, HEADS)
            act.activation(h_hi[:, HEADS - 1], og[:, HEADS - 1], ACT.Copy).then_inc(g_hi, 1)

        def pool_mixer(pool):
            def exponents(i, n):
                if n < 2:
                    if not (isinstance(i, int) and i == 0):
                        pool.wait_ge(m_ops, 8 * i + n - 1)
                else:
                    pool.wait_ge(m_ops, 8 * i + n - 1)
                if n == NL:
                    c3 = cum[:].rearrange("p (c t) -> p c t", t=P)
                    pool.tensor_tensor(decay[:, n % 2].rearrange("p (c t) -> p c t", t=P),
                                       c3[:, :, P - 1:P].broadcast_to([P, NC, P]), c3,
                                       ALU.subtract).then_inc(m_dif, 1)
                    return
                b = LEVELS[n]
                c4 = blocks(cum[:], b)
                ref = c4[:, :, 0, b - 1:b].broadcast_to([P, HALF // b, b])
                lo = decay[:, n % 2, LO].rearrange("p (a b) -> p a b", b=b)
                up = decay[:, n % 2, UP].rearrange("p (a b) -> p a b", b=b)
                if b > 1:
                    pool.tensor_tensor(lo, ref, c4[:, :, 0, :], ALU.subtract)
                pool.tensor_tensor(up, c4[:, :, 1, :], ref, ALU.subtract).then_inc(m_dif, 1)

            def step(i, first=False):
                n = MIX0 + 4 * i
                if not first:
                    split_lo_col(pool, n + 1, 1)
                split_lo_col(pool, n + 2, 2)
                pool.wait_ge(m_cum, i + 1)
                exponents(i, 0)
                exponents(i, 1)
                split_lo_col(pool, n + 3, 3)
                for m in (2, 3, 4):
                    exponents(i, m)
                split_lo_col(pool, n + 4, 0)
                for m in (5, 6, 7):
                    exponents(i, m)

            step(0, True)
            with pool.Fori(1, HEADS) as i:
                step(i)
            split_lo_col(pool, OUT0 + 1, 1)

        def dve_mixer(dve):
            def state_chain(h):
                dve.wait_ge(m_upd, h + 1)
                dve.wait_ge(m_tdec, h + 1)
                dve.tensor_copy(state[:, 1], small[:, 0:P]).then_inc(m_state, 1)
                for c in range(1, NC - 1):
                    dve.wait_ge(m_state, 7 * h + c)
                    dve.scalar_tensor_tensor(out=state[:, c + 1], in0=state[:, c],
                                             scalar=tile_dec[:, c:c + 1],
                                             in1=small[:, c * P:(c + 1) * P],
                                             op0=ALU.mult, op1=ALU.add).then_inc(m_state, 1)

            def gate(h):
                dve.wait_ge(m_hrstd, h + 1)
                dve.scalar_tensor_tensor(out=sig_q[:], in0=bank[3][:],
                                         scalar=gains[:, V_HEAD:V_HEAD + 1], in1=sig_q[:],
                                         op0=ALU.mult, op1=ALU.mult).then_inc(m_norm, 1)
                dve.wait_ge(m_og, h + 1)
                dve.wait_ge(m_norm, h + 1)
                dve.tensor_tensor(og[:, bass.ds(h, 1)], og[:, bass.ds(h, 1)],
                                  sig_q[:].rearrange("p (o t) -> p o t", o=1),
                                  ALU.mult).then_inc(m_gated, 1)

            def operands(i, n):
                dve.wait_ge(m_exp, 8 * i + n + 1)
                if n == NL:
                    dve.tensor_tensor(k_end[:], k_t[:], decay[:, n % 2], ALU.mult).then_inc(m_ops, 1)
                    return
                if n >= 2:
                    dve.wait_ge(m_lvl, 9 * i + n - 1)
                b = LEVELS[n]
                if b > 1:
                    dve.tensor_tensor(blocks(k_dec[:, n % 2], b)[:, :, 0, :], blocks(k_t[:], b)[:, :, 0, :],
                                      decay[:, n % 2, LO].rearrange("p (a b) -> p a b", b=b), ALU.mult)
                dve.tensor_tensor(q_dec[:, n % 2].rearrange("p (a b) -> p a b", b=b),
                                  blocks(q_t[:], b)[:, :, 1, :],
                                  decay[:, n % 2, UP].rearrange("p (a b) -> p a b", b=b),
                                  ALU.mult).then_inc(m_ops, 1)

            def select(i, n):
                if not (isinstance(i, int) and i == 0 and n == 0):
                    dve.wait_ge(m_sel, 9 * i + n)
                dve.wait_ge(m_lvl, 9 * i + n + 1)
                dve.sem_inc(m_seen, 1)
                if n < NL:
                    b = LEVELS[n]
                    off = (n % 2) * HALF
                    dve.copy_predicated(
                        blocks(scores[:], b)[:, :, 1, :],
                        masks[:, n:n + 1, :].bitcast(U32).rearrange("p o (a b) -> p o a b", b=b)
                        .broadcast_to([P, NC, 64 // b, b]),
                        small[:, off:off + HALF].rearrange("p (c a b) -> p c a b", c=NC, b=b),
                    ).then_inc(m_sel, 1)
                else:
                    half = n - NL
                    place = (small[:, UP], bank[3][:, LO])[half]
                    dve.copy_predicated(
                        scores[:, half * HALF:(half + 1) * HALF].rearrange("p (c t) -> p c t", t=P),
                        ident[:].bitcast(U32).rearrange("p (o t) -> p o t", o=1).broadcast_to([P, 4, P]),
                        place.rearrange("p (c t) -> p c t", t=P),
                    ).then_inc(m_sel, 1)

            def step(i, first=False):
                n = MIX0 + 4 * i
                if not first:
                    dve.wait_ge(m_kturn, 2 * i)
                dve.wait_ge(m_sigf, i + 1)
                dve.tensor_scalar(k_t[:], sig_a[:], lbv[:, L_MINUS, bass.ds(i, 1)],
                                  lbv[:, L_ONE_MINUS, bass.ds(i, 1)], ALU.mult, ALU.add).then_inc(m_k, 1)
                if not first:
                    state_chain(i - 1)
                dve.wait_ge(m_logf, i + 1)
                for c in range(NC):
                    s = slice(c * P, (c + 1) * P)
                    cs = dve.tensor_tensor_scan(cum[:, s], ones[:], logf[:, s], 0.0, ALU.mult, ALU.add)
                cs.then_inc(m_cum, 1)
                dve.wait_ge(m_sigq, i + 1)
                dve.scalar_tensor_tensor(out=q_t[:], in0=sig_q[:], scalar=QSCALE, in1=bank[1][:],
                                         op0=ALU.mult, op1=ALU.mult).then_inc(m_q, 1)
                dve.wait_ge(m_q, i + 1)
                operands(i, 0)
                operands(i, 1)
                for m in range(2, NL):
                    select(i, m - 2)
                    operands(i, m)
                    if m == 3 and not first:
                        gate(i - 1)
                select(i, NL - 2)
                operands(i, NL)
                dve.wait_ge(m_qexp, i + 1)
                dve.tensor_tensor(q_cum[:], q_cum[:], q_t[:], ALU.mult).then_inc(m_qcum, 1)
                dve.wait_ge(m_sigg, i + 1)
                if first:
                    dve.wait_ge(s_park, 16)
                dve.tensor_tensor(og[:, bass.ds(i, 1)], sig_a[:].rearrange("p (o t) -> p o t", o=1),
                                  bank[1][:].rearrange("p (o t) -> p o t", o=1),
                                  ALU.mult).then_inc(m_og, 1)
                for m in (6, 7, 8):
                    select(i, m)

            dve.memset(scores[:], 0.0).then_inc(m_zero, 1)
            dve.memset(k_dec[:], 0.0).then_inc(m_zero, 1)
            dve.wait_ge(m_zero, 2)
            step(0, True)
            with dve.Fori(1, HEADS) as i:
                step(i)
            state_chain(HEADS - 1)

            def gated_lo(h):
                dve.wait_ge(g_hi, h + 1)
                dve.tensor_tensor(h_lo[:, h], og[:, h], h_hi[:, h].bitcast(F32),
                                  ALU.subtract).then_inc(g_lo, 1)

            for h in range(HEADS - 1):
                gated_lo(h)
            gate(HEADS - 1)
            gated_lo(HEADS - 1)

        def act_out(act, nm):
            for d in range(DT - 2):
                split_hi_col(act, OUT0 + d + 2, (d + 2) % 4)
                act_square(act, nm, 0, d, o_add, d + 1)
            act_square(act, nm, 0, 6, o_add, 7)
            act_square(act, nm, 0, 7, o_add, 8)
            for d in range(DT - 2):
                act_square(act, nm, 1, d)
            for n in (FFN0, FFN0 + 1):
                split_hi_col(act, n, n % 4, False, ffn_b.first_split[0])
            act_rstd(act, nm, 0, bank[1])
            for d in range(4):
                act_h_hi(act, nm, 0, d)
            act_square(act, nm, 1, 6, o_add, 9)
            for d in (4, 5):
                act_h_hi(act, nm, 0, d)
            act_square(act, nm, 1, 7, o_add, 10)
            for d in (6, 7):
                act_h_hi(act, nm, 0, d)
            act_rstd(act, nm, 1, bank[2])
            for d in range(DT):
                act_h_hi(act, nm, 1, d)

        def dve_out(dve, nm, which):
            def x_add(d, s):
                dve.tensor_tensor(xT[:, d, s], xT[:, d, s], bank[d % 4][:, s], ALU.add).then_inc(o_add, 1)

            for d in range(DT - 2):
                dve.wait_ge(s_cdone, OUT0 + d + 1)
                dve.wait_ge(s_back[d], 16)
                x_add(d, slice(0, T))
                if d:
                    dve_add_square(dve, nm, 0, d - 1)
            for u, d in enumerate((DT - 2, DT - 1)):
                dve.wait_ge(o_last, u + 1)
                dve.wait_ge(s_back[d], 16)
                x_add(d, BOTH[0])
                dve_add_square(dve, nm, 0, d - 1)
            dve_add_square(dve, nm, 0, DT - 1)
            for d in range(DT - 2):
                dve_add_square(dve, nm, 1, d)
            for d in range(4):
                dve_h_tile(dve, nm, which, 0, d)
            for d, turns in ((DT - 2, (4, 5)), (DT - 1, (6, 7))):
                dve.wait_ge(s_cdone, OUT0 + d + 1)
                x_add(d, BOTH[1])
                dve_add_square(dve, nm, 1, d)
                for t in turns:
                    dve_h_tile(dve, nm, which, 0, t)
            for d in range(DT):
                dve_h_tile(dve, nm, which, 1, d)

        def act_gain(eng, c, d):
            s = BOTH[c]
            eng.activation(xT[:, d, s], xT[:, d, s], ACT.Copy,
                           scale=gains[:, V_FINAL + d:V_FINAL + d + 1]).then_inc(s_gained, 1)

        def pool_final(eng):
            done = 0
            for c in range(2):
                for d in range(DVE_SCALES[c], DT):
                    done += 1
                    eng.wait_ge(norms[3].rstd, c + 1)
                    eng.wait_ge(s_gained, done)
                    eng.tensor_tensor(xT[:, d, BOTH[c]], xT[:, d, BOTH[c]], rstd[:, BOTH[c]],
                                      ALU.mult).then_inc(s_final[1], 1)

        @block.sync
        def _(sp):
            sp.dma_start(vec_rows[V_NORM:V_FINAL], norm_gains[0].rearrange("w (a p) -> (w a) p", p=P)).then_inc(s_vec, 16)
            sp.dma_start(vec_rows[V_FINAL:V_LOGIT0], final_gain.rearrange("(a p) -> a p", p=P)).then_inc(s_vec, 16)
            sp.dma_start(vec_rows[V_LOGIT0:V_HEAD], lb_logits.rearrange("w (a p) -> (w a) p", p=P)).then_inc(s_vec, 16)
            sp.dma_start(vec_rows[V_HEAD:NVEC], head_gain).then_inc(s_vec, 16)
            for t in range(NC):
                if t >= 4:
                    sp.wait_ge(s_turned, t - 3)
                sp.dma_start(stage[:, t % 4], x[0, t * P:(t + 1) * P, :]).then_inc(s_xload[t % 4], 16)
            sp_ffn(sp, ffn_a)
            sp_mixer(sp)
            sp.wait_ge(s_park, 16)
            for d in range(4):
                load_col(sp, w_out[0][:, d * P:(d + 1) * P], OUT0 + d, d)
            for d in range(DT):
                sp.wait_ge(g_lo, d + 1)
                sp.dma_start(xT[:, d], x_park[:, d * T:(d + 1) * T]).then_inc(s_back[d], 16)
            for d in range(4, DT):
                load_col(sp, w_out[0][:, d * P:(d + 1) * P], OUT0 + d, d % 4)
            sp_ffn(sp, ffn_b)
            for t in range(NC):
                sp.wait_ge(s_placed_out[t % 2], t // 2 + 1)
                sp.dma_start(out[0, t * P:(t + 1) * P, :], stage[:, t % 4]).then_inc(s_out[t % 4], 16)
            for done in s_out:
                sp.wait_ge(done, 16 * NC // 4)

        @block.gpsimd
        def _(pool):
            pool.memset(ones[:], 1.0).then_inc(s_ones, 1)
            pool.memset(eps[:], EPS).then_inc(s_eps, 1)
            pool.memset(ident[:], 0.0).then_inc(s_ident, 1)
            pool.memset(masks[:], 1.0).then_inc(s_mask, 1)
            pool.wait_ge(s_ident, 1)
            pool.affine_select(out=ident[:], in_=ident[:], compare_op=ALU.not_equal, fill=1.0, base=0,
                               pattern=[[-1, P]], channel_multiplier=1).then_inc(s_ident, 1)
            for n, b in enumerate(LEVELS):
                m = masks[:, n].rearrange("p (a b) -> p a b", b=b)
                pool.wait_ge(s_mask, 2 * n + 1)
                pool.affine_select(out=m, in_=m, compare_op=ALU.is_ge, fill=0.0, base=0,
                                   pattern=[[-2 * b, 64 // b], [0, b]], channel_multiplier=1).then_inc(s_mask, 1)
                pool.wait_ge(s_mask, 2 * n + 2)
                pool.affine_select(out=m, in_=m, compare_op=ALU.is_ge, fill=0.0, base=b - 1,
                                   pattern=[[2 * b, 64 // b], [0, b]], channel_multiplier=-1).then_inc(s_mask, 1)
            split_lo_col(pool, 0, 0)
            split_lo_col(pool, 1, 1)
            pool_norm(pool, norms[0])
            pool_ffn(pool, ffn_a)
            split_lo_col(pool, MIX0, 0)
            split_lo_col(pool, MIX0 + 1, 1)
            pool_norm(pool, norms[1])
            pool_mixer(pool)
            for n in range(OUT0 + 2, FFN0):
                split_lo_col(pool, n, n % 4)
            for n in (FFN0, FFN0 + 1):
                split_lo_col(pool, n, n % 4, *ffn_b.first_split)
            pool_norm(pool, norms[2])
            pool_ffn(pool, ffn_b)
            pool_final(pool)

        @block.scalar
        def _(act):
            act.wait_ge(s_lb, 3)
            act.activation(lbv[:, L_E0:L_E1 + 1], lbv[:, L_E0:L_E1 + 1], ACT.Exp).then_inc(s_lbexp, 1)
            def place(t):
                act.wait_ge(s_turned, t + 1)
                act.activation(xT[:, :, t * P:(t + 1) * P], bank[1][:].rearrange("p (d t) -> p d t", t=P),
                               ACT.Copy).then_inc(s_placed[1], 1)

            place(1)
            place(3)
            act.wait_ge(s_placed[0], NC // 4)
            act.wait_ge(s_placed[1], NC // 4)
            for d in range(DT):
                act_square(act, norms[0], 0, d)
                if d == 1:
                    place(5)
                if d == 4:
                    place(7)
            split_hi_col(act, 0, 0, False)
            split_hi_col(act, 1, 1, False)
            act.wait_ge(s_eps, 1)
            act_rstd(act, norms[0], 0, bank[2])
            act.wait_ge(s_placed[0], NC // 2)
            act.wait_ge(s_placed[1], NC // 2)
            for d in range(DT):
                act_h_hi(act, norms[0], 0, d)
                act_square(act, norms[0], 1, d)
            act_rstd(act, norms[0], 1, bank[2])
            for d in range(DT):
                act_h_hi(act, norms[0], 1, d)
            act_ffn(act, ffn_a)
            act_norm_after(act, norms[1], ffn_a.xadd, DT * (GROUPS - 1), MIX0)
            act_mixer(act)
            act_out(act, norms[2])
            act_ffn(act, ffn_b)
            act_norm_after(act, norms[3], ffn_b.xadd, DT * (GROUPS - 1), None)
            for t in range(1, NC, 2):
                if t >= 4:
                    act.wait_ge(s_out[t % 4], 16)
                act.wait_ge(s_outturn, t + 1)
                act.activation(stage[:, t % 4], bank[t % 2][:], ACT.Copy).then_inc(s_placed_out[1], 1)

        @block.vector
        def _(dve):
            dve.wait_ge(s_vturn, 1)
            dve.tensor_copy(gains[:], bank[2][:, 0:NVEC]).then_inc(s_gains, 1)
            dve.wait_ge(s_gains, 1)
            l0, l1 = gains[:, V_LOGIT0:V_LOGIT1], gains[:, V_LOGIT1:V_HEAD]
            dve.tensor_tensor(lbv[:, L_MAX], l0, l1, ALU.max).then_inc(s_lb, 1)
            dve.wait_ge(s_lb, 1)
            dve.tensor_tensor(lbv[:, L_E0], l0, lbv[:, L_MAX], ALU.subtract).then_inc(s_lb, 1)
            dve.tensor_tensor(lbv[:, L_E1], l1, lbv[:, L_MAX], ALU.subtract).then_inc(s_lb, 1)

            def place(t):
                dve.wait_ge(s_turned, t + 1)
                dve.tensor_copy(xT[:, :, t * P:(t + 1) * P],
                                bank[0][:].rearrange("p (d t) -> p d t", t=P)).then_inc(s_placed[0], 1)

            place(0)
            place(2)
            dve.wait_ge(s_lbexp, 1)
            dve.tensor_tensor(lbv[:, L_SUM], lbv[:, L_E0], lbv[:, L_E1], ALU.add).then_inc(s_lb, 1)
            dve.wait_ge(s_lb, 4)
            dve.reciprocal(lbv[:, L_INV], lbv[:, L_SUM]).then_inc(s_lb, 1)
            dve.wait_ge(s_lb, 5)
            dve.tensor_tensor(lbv[:, L_LB], lbv[:, L_E0], lbv[:, L_INV], ALU.mult).then_inc(s_lb, 1)
            dve.wait_ge(s_lb, 6)
            dve.tensor_scalar(lbv[:, L_ONE_MINUS], lbv[:, L_LB], -1.0, 1.0, ALU.mult, ALU.add).then_inc(s_lb, 1)
            dve.tensor_scalar(lbv[:, L_MINUS], lbv[:, L_LB], 1.0, None, ALU.subtract).then_inc(s_lb, 1)
            dve.wait_ge(s_lb, 8)
            dve.tensor_scalar(lbv[:, L_LB], lbv[:, L_LB], TINY, None, ALU.max).then_inc(s_lb, 1)
            dve.wait_ge(s_lb, 9)
            for d in range(DT):
                dve_add_square(dve, norms[0], 0, d)
                if d == 1:
                    place(4)
                if d == 4:
                    place(6)
            for d in range(DT):
                dve_h_tile(dve, norms[0], 0, 0, d)
                if d:
                    dve_add_square(dve, norms[0], 1, d - 1)
            dve_add_square(dve, norms[0], 1, DT - 1)
            for d in range(DT):
                dve_h_tile(dve, norms[0], 0, 1, d)
            dve_ffn(dve, ffn_a, lambda c, d: dve_h_tile(dve, norms[1], 1, c, d))
            dve.wait_ge(s_ones, 1)
            dve.wait_ge(s_ident, 2)
            dve.wait_ge(s_mask, 2 * NL + 1)
            dve_mixer(dve)
            dve_out(dve, norms[2], 2)

            def place_out(t):
                if t >= 4:
                    dve.wait_ge(s_out[t % 4], 16)
                dve.wait_ge(s_outturn, t + 1)
                dve.tensor_copy(stage[:, t % 4], bank[t % 2][:]).then_inc(s_placed_out[0], 1)

            def scale_turn(c, d):
                if (c, d) == (1, 0):
                    place_out(0)
                    place_out(2)
                if d < DVE_SCALES[c]:
                    dve.wait_ge(norms[3].rstd, c + 1)
                    dve.scalar_tensor_tensor(out=xT[:, d, BOTH[c]], in0=xT[:, d, BOTH[c]],
                                             scalar=gains[:, V_FINAL + d:V_FINAL + d + 1],
                                             in1=rstd[:, BOTH[c]], op0=ALU.mult,
                                             op1=ALU.mult).then_inc(s_final[0], 1)

            dve_ffn(dve, ffn_b, scale_turn)
            place_out(4)
            place_out(6)

        @block.tensor
        def _(pe):
            pe.wait_ge(s_ident, 2)
            pe.wait_ge(s_vec, 64)
            pe.transpose(bank[2][:, 0:NVEC], vec_rows[:], ident[0:NVEC, 0:NVEC]).then_inc(s_vturn, 1)
            for t in range(NC):
                pe.wait_ge(s_xload[t % 4], 16 * (t // 4 + 1))
                if t >= 2:
                    pe.wait_ge(s_placed[t % 2], t // 2)
                for d in range(DT):
                    mm = pe.transpose(bank[t % 2][:, d * P:(d + 1) * P], stage[:, t % 4, d * P:(d + 1) * P],
                                      ident[:])
                mm.then_inc(s_turned, 1)
                if t == NC - 1:
                    pe.wait_ge(s_ones, 1)
                    pe.wait_ge(s_gains, 1)
                    pe_norm_sum(pe, norms[0], 0, bank[2])
            for placed in s_placed:
                pe.wait_ge(placed, NC // 2)
            pe_ffn(pe, ffn_a)
            pe_mixer(pe)
            for d in range(2, DT - 2):
                if d >= 4:
                    pe.wait_ge(o_add, d - 3)
                pe_col_unit(pe, OUT0 + d, d % 4, bank[d % 4])
            for c in range(2):
                for d in (DT - 2, DT - 1):
                    if c == 0:
                        pe.wait_ge(s_clo, OUT0 + d + 1)
                        pe.wait_ge(o_add, d - 3)
                    for k in range(DT):
                        mm = pe_col_tile(pe, d, k, bank[d % 4], (BOTH[c],))
                        if k == DT - 1:
                            mm.then_inc(o_last if c == 0 else s_cdone, 1)
                        if c == 1 and d == DT - 2 and k == 3:
                            pe_norm_sum(pe, norms[2], 0, bank[1])
            pe_ffn(pe, ffn_b)
            pe_norm_sum(pe, norms[3], 1, bank[2])
            for t in range(NC):
                if t >= 2:
                    pe.wait_ge(s_placed_out[t % 2], t // 2)
                for d in range(DT):
                    if t % 4 == 0:
                        by_dve = DVE_SCALES[t // 4]
                        if d < by_dve:
                            pe.wait_ge(s_final[0], (t // 4) * DVE_SCALES[0] + d + 1)
                        else:
                            pe.wait_ge(s_final[1], (t // 4) * (DT - DVE_SCALES[0]) + d - by_dve + 1)
                    mm = pe.transpose(bank[t % 2][:, d * P:(d + 1) * P], xT[:, d, t * P:(t + 1) * P],
                                      ident[:])
                mm.then_inc(s_outturn, 1)


_INS = ['x', 'ffn_w_gate_up', 'ffn_w_down', 'norm_gains', 'final_norm_gain', 'hgrn_w_in',
        'hgrn_lower_bound_logits', 'hgrn_norm_gain', 'hgrn_w_out']


def kernel(**inputs):
    import numpy as np
    import concourse.bacc as bacc
    from concourse.bass_utils import run_bass_kernel_spmd

    nc = bacc.Bacc("TRN2", target_bir_lowering=False, num_devices=1)
    arrays, args = {}, []
    for name in _INS:
        a = np.ascontiguousarray(inputs[name])
        arrays[f"in_{name}"] = a
        args.append(nc.dram_tensor(f"in_{name}", a.shape, mybir.dt.from_np(a.dtype), kind="ExternalInput").ap())
    args.append(nc.dram_tensor("trunk_out", (1, T, D), F32, kind="ExternalOutput").ap())
    hgrn2_trunk(nc, *args)
    r = run_bass_kernel_spmd(nc, [arrays], core_ids=[0])
    return r.results[0]["trunk_out"]
```

```python
from contextlib import ExitStack

import concourse.bass as bass
from concourse import mybir

F32 = mybir.dt.float32
F32R = mybir.dt.float32r
U32 = mybir.dt.uint32
ALU = mybir.AluOpType
ACT = mybir.ActivationFunctionType

P = 128
T = 1024
HALF = 512
LO, UP = slice(0, HALF), slice(HALF, T)
BOTH = (LO, UP)
D = 1024
DT = D // P
FF = 2816
FT = FF // P
GROUPS = FT // 2
HEADS = 8
NC = T // P
ROUNDS = (32, 8, 2)
NR = len(ROUNDS)
Q_LEN = tuple((3 - j) * P // 4 for j in range(3))
Q_OFF = tuple(sum(Q_LEN[:j]) for j in range(3))
QW = sum(Q_LEN)
Q_ALL = NC * QW
PW = 256
HALVES = 2 * (NR + 1)
SEL = 3 * 2 * NR + 4
OPS = NR + 2
MASKS = tuple((b, b) for b in ROUNDS) + ((1, 2),)
M_OFF = tuple(sum(P // step for _, step in MASKS[:n]) for n in range(len(MASKS) + 1))
HD = D // HEADS
QSCALE = float(HD) ** -0.5
EPS = 1e-6
V_NORM, V_FINAL, V_LOGIT0, V_LOGIT1, V_HEAD = 0, 3 * DT, 4 * DT, 5 * DT, 6 * DT
NVEC = V_HEAD + 1
L_MAX, L_E0, L_E1, L_SUM, L_INV, L_LB, L_ONE_MINUS, L_MINUS = range(8)
LN_EXP = "natural_log_exp_and_others"
TINY = 2.0 ** -60


def hgrn2_trunk(nc, x, w_gate_up, w_down, norm_gains, final_gain, w_in, lb_logits, head_gain,
                w_out, out):
    ctx = ExitStack()
    with ctx:
        def sb(stack, name, shape, dt=F32):
            return stack.enter_context(nc.sbuf_tensor(name, shape, dt))

        def sem(name):
            return ctx.enter_context(nc.semaphore(name))

        h_hi = sb(ctx, "h_hi", [P, DT, T], F32R)
        h_lo = sb(ctx, "h_lo", [P, DT, T], F32R)
        col_hi = sb(ctx, "col_hi", [P, 2, DT, P], F32R)
        col_lo = sb(ctx, "col_lo", [P, 2, DT, P], F32R)
        col_raw = sb(ctx, "col_raw", [P, 4, DT, P])
        ident = sb(ctx, "ident", [P, P])
        ones = sb(ctx, "ones", [P, P])
        ones_r = sb(ctx, "ones_r", [P, P], F32R)
        masks = sb(ctx, "masks", [P, M_OFF[-1]])
        gains = sb(ctx, "gains", [P, NVEC])
        lbv = sb(ctx, "lbv", [P, 8, HEADS])
        vec_rows = sb(ctx, "vec_rows", [NVEC, P])
        eps = sb(ctx, "eps", [P, 1])

        ffn_mem = ExitStack()
        xT = sb(ffn_mem, "xT", [P, DT, T])
        sumsq = sb(ffn_mem, "sumsq", [P, T])
        rstd = sb(ffn_mem, "rstd", [P, T])
        act_hi = sb(ffn_mem, "act_hi", [P, 2, T], F32R)
        act_lo = sb(ffn_mem, "act_lo", [P, 2, T], F32R)
        row_hi = sb(ffn_mem, "row_hi", [P, 2, D], F32R)
        row_lo = sb(ffn_mem, "row_lo", [P, 2, D], F32R)
        row_raw = sb(ffn_mem, "row_raw", [P, 2, D])
        silu_g = sb(ffn_mem, "silu_g", [P, T])
        prod = sb(ffn_mem, "prod", [P, T])
        stage = sb(ffn_mem, "stage", [P, 4, D])
        ffn_mem.close()

        mix_mem = ExitStack()
        og = sb(mix_mem, "og", [P, HEADS, T])
        sig_a = sb(mix_mem, "sig_a", [P, T])
        sig_q = sb(mix_mem, "sig_q", [P, T])
        logf = sb(mix_mem, "logf", [P, T])
        cum = sb(mix_mem, "cum", [P, T])
        k_t = sb(mix_mem, "k_t", [P, T])
        q_all = sb(mix_mem, "q_all", [P, NC, QW])
        work = sb(mix_mem, "work", [P, 2, T + Q_ALL])
        q_cum = sb(mix_mem, "q_cum", [P, T])
        scores = sb(mix_mem, "scores", [P, T])
        tile_dec = sb(mix_mem, "tile_dec", [P, NC])
        k_end = sb(mix_mem, "k_end", [P, T])
        k_nat = sb(mix_mem, "k_nat", [P, NC, P])
        v_nat = sb(mix_mem, "v_nat", [P, NC, P])
        state = sb(mix_mem, "state", [P, NC, P])
        v_t = sb(mix_mem, "v_t", [P, T])
        mix_mem.close()

        first_mem = ExitStack()
        sb(first_mem, "below_mix_first", [P, 21 * T + Q_ALL + NC])
        mix_first = (sb(first_mem, "mix_first_hi", [P, 2, DT, P], F32R),
                     sb(first_mem, "mix_first_lo", [P, 2, DT, P], F32R))
        first_mem.close()

        squares_mem = ExitStack()
        sb(squares_mem, "below_logf", [P, 10 * T])
        osq_lo = sb(squares_mem, "osq_lo", [P, T], F32R)
        sb(squares_mem, "logf_to_v_t", [P, 13 * T + Q_ALL + NC])
        osq_hi = sb(squares_mem, "osq_hi", [P, T], F32R)
        squares_mem.close()

        bank = [ctx.enter_context(nc.psum_tensor(f"bank{i}", [P, T], F32)) for i in range(4)]

        x_park = nc.dram_tensor("x_park", (P, DT * T), F32, kind="Internal").ap()

        block = ctx.enter_context(nc.Block())

        s_xload = [sem(f"x_rows_loaded{i}") for i in range(4)]
        s_vec = sem("vectors_loaded")
        s_ident = sem("identity_steps")
        s_ones = sem("ones_made")
        s_mask = sem("mask_steps")
        s_eps = sem("eps_made")
        s_turned = sem("x_tiles_turned")
        s_placed = [sem("x_placed_by_vector"), sem("x_placed_by_scalar")]
        s_vturn = sem("vectors_turned")
        s_gains = sem("gains_placed")
        s_lb = sem("lower_bound_steps")
        s_lbexp = sem("lower_bound_exps")
        s_cload = [sem(f"col_loaded{i}") for i in range(4)]
        s_chi = sem("col_hi_made")
        s_clo = sem("col_lo_made")
        s_cdone = sem("col_units_done")
        s_park = sem("x_parked")
        s_back = [sem(f"x_back{d}") for d in range(DT)]
        s_gained = sem("x_times_gain")
        s_final = [sem("x_scaled_by_vector"), sem("x_scaled_by_gpsimd")]
        s_outturn = sem("out_tiles_turned")
        s_placed_out = [sem("out_rows_by_vector"), sem("out_rows_by_scalar")]
        s_out = [sem(f"rows_written{i}") for i in range(4)]

        class Norm:

            def __init__(self, tag):
                self.squared = sem(f"{tag}_squared")
                self.added = sem(f"{tag}_added")
                self.summed = sem(f"{tag}_summed")
                self.log = sem(f"{tag}_log")
                self.rstd = sem(f"{tag}_rstd")
                self.scaled = sem(f"{tag}_scaled")
                self.hi = sem(f"{tag}_hi")
                self.lo = [sem(f"{tag}_lo_even"), sem(f"{tag}_lo_odd")]

        class Ffn:
            def __init__(self, tag, which, slot0, norm, after):
                self.which, self.slot0 = which, slot0
                self.norm, self.after = norm, after
                self.rload = [sem(f"{tag}_row_loaded{i}") for i in range(2)]
                self.rhi = sem(f"{tag}_row_hi_made")
                self.rlo = sem(f"{tag}_row_lo_made")
                self.silu = sem(f"{tag}_silu_made")
                self.prod = sem(f"{tag}_prod_made")
                self.ahi = sem(f"{tag}_act_hi_made")
                self.alo = sem(f"{tag}_act_lo_made")
                self.down = sem(f"{tag}_down_done")
                self.xadd = sem(f"{tag}_x_added")
                self.last_up = sem(f"{tag}_last_up_first_half")
                self.last_prod = sem(f"{tag}_last_prod_halves")
                self.last_ahi = sem(f"{tag}_last_act_hi_halves")
                self.last_alo = sem(f"{tag}_last_act_lo_halves")

        norms = [Norm(f"norm{i}") for i in range(4)]
        MIX0 = 4 * GROUPS
        OUT0 = MIX0 + 4 * HEADS
        FFN0 = OUT0 + DT
        rows_as_cols = [row[:].rearrange("p t (k c) -> p t k c", c=P) for row in (row_hi, row_lo)]
        ffn_a = Ffn("ffn_a", 0, 0, norms[0], norms[1])
        ffn_b = Ffn("ffn_b", 1, FFN0, norms[2], norms[3])

        m_sigf = sem("m_sigmoid_f")
        m_logf = sem("m_log_f")
        m_k = sem("m_k_made")
        m_cum = sem("m_cum_made")
        m_tdec = sem("m_tile_decay")
        m_sigq = sem("m_sigmoid_q")
        m_q = sem("m_q_made")
        m_vt = sem("m_v_copied")
        m_sigg = sem("m_sigmoid_g")
        m_og = sem("m_out_gate")
        m_dif = sem("m_exponent_made")
        m_exp = sem("m_decay_made")
        m_ops = sem("m_decayed_operands")
        m_lvl = sem("m_scores_done")
        m_sel = sem("m_scores_selected")
        m_vturn = sem("m_v_turned")
        m_vnat = sem("m_v_rows")
        m_kturn = sem("m_k_turned")
        m_knat = sem("m_k_rows")
        m_qexp = sem("m_exp_cum")
        m_qcum = sem("m_q_cum")
        m_upd = sem("m_state_products")
        m_state = sem("m_state_steps")
        m_o = sem("m_o_done")
        m_osq = sem("m_o_squared")
        m_osq_hi = sem("m_o_squared_hi")
        m_osq_lo = sem("m_o_squared_lo")
        m_osum = sem("m_o_summed")
        m_hlog = sem("m_head_log")
        m_hrstd = sem("m_head_rstd")
        m_norm = sem("m_o_normed")
        m_gated = sem("m_gated")
        m_zero = sem("m_buffers_zeroed")
        m_seen = sem("m_level_wait_passed")
        s_seen = sem("load_wait_passed")
        g_hi = sem("gated_hi_made")
        g_lo_first = sem("gated_lo_made_of_head_0")
        g_lo = sem("gated_lo_made")
        o_last = sem("mixer_last_units_first_half")
        o_add = sem("mixer_x_added")

        def addr(eng, value):
            return value if isinstance(value, int) else eng.snap(value)

        def load_col(eng, src, n, r, started=True, alone=False):
            if started:
                eng.wait_ge(s_clo, n - 3)
            if alone:
                eng.sem_inc(s_seen, 1)
            eng.dma_start(col_raw[:, r], src.rearrange("(k p) c -> p k c", p=P)).then_inc(s_cload[r], 16)

        def split_hi_col(eng, n, r, started=True, hi=col_hi, back=2):
            eng.wait_ge(s_cload[r], (n - r) * 4 + 16)
            if started:
                eng.wait_ge(s_cdone, n - back + 1)
            eng.activation(hi[:, r % 2], col_raw[:, r], ACT.Copy).then_inc(s_chi, 1)

        def split_lo_col(eng, n, r, hi=col_hi, lo=col_lo):
            eng.wait_ge(s_chi, n + 1)
            eng.tensor_tensor(lo[:, r % 2], col_raw[:, r], hi[:, r % 2].bitcast(F32),
                              ALU.subtract).then_inc(s_clo, 1)

        def pe_three(eng, dst, w_hi, w_lo, a_hi, a_lo, first, last, over=BOTH):
            for n, a in enumerate((a_hi, a_lo)):
                for s in over:
                    eng.matmul(dst[:, s], w_hi, a[:, s], start=first and n == 0, stop=False)
            for s in over:
                mm = eng.matmul(dst[:, s], w_lo, a_hi[:, s], start=False, stop=last)
            return mm

        def pe_col_tile(eng, r, k, dst, over=BOTH, split=(col_hi, col_lo)):
            return pe_three(eng, dst, split[0][:, r % 2, k], split[1][:, r % 2, k], h_hi[:, k], h_lo[:, k],
                            k == 0, k == DT - 1, over)

        def pe_col_unit(eng, n, r, dst, between=None):
            eng.wait_ge(s_clo, n + 1)
            for k in range(DT):
                mm = pe_col_tile(eng, r, k, dst)
                if k == DT - 1:
                    mm.then_inc(s_cdone, 1)
                if between:
                    between(k)

        def pe_first_units(eng, n, nm, split, sum_after=3):
            for c, s in enumerate(BOTH):
                for k in range(DT):
                    eng.wait_ge(nm.lo[k % 2], 4 * c + k // 2 + 1)
                    for u in range(2):
                        if c == 0 and k == 0:
                            eng.wait_ge(s_clo, n + u + 1)
                        mm = pe_col_tile(eng, u, k, bank[u], (s,), split)
                        if c == 1 and k == DT - 1:
                            mm.then_inc(s_cdone, 1)
                    if c == 0 and k == sum_after:
                        pe_norm_sum(eng, nm, 1, bank[2])

        sq_buf = (silu_g, prod)

        def act_square(eng, nm, c, d, ready=None, count=None):
            if ready is not None:
                eng.wait_ge(ready, count)
            q = DT * c + d
            if d >= 2:
                eng.wait_ge(nm.added, q - 1)
            eng.activation(sq_buf[d % 2][:, BOTH[c]], xT[:, d, BOTH[c]], ACT.Square).then_inc(nm.squared, 1)

        def dve_add_square(eng, nm, c, d):
            q = DT * c + d
            s = BOTH[c]
            eng.wait_ge(nm.squared, q + 1)
            if d:
                eng.wait_ge(nm.added, q)
                eng.tensor_tensor(sumsq[:, s], sumsq[:, s], sq_buf[d % 2][:, s], ALU.add).then_inc(nm.added, 1)
            else:
                eng.tensor_copy(sumsq[:, s], sq_buf[0][:, s]).then_inc(nm.added, 1)

        def pe_norm_sum(eng, nm, c, dst):
            eng.wait_ge(nm.added, DT * (c + 1))
            eng.matmul(dst[:, BOTH[c]], ones[:], sumsq[:, BOTH[c]], start=True, stop=True).then_inc(nm.summed, 1)

        def pe_square_sum(eng, nm, dst, tiles):
            for d in tiles:
                eng.wait_ge(nm.squared, d + 1)
                eng.matmul(dst[:, LO], ones[:], sq_buf[d % 2][:, LO],
                           start=d == 0, stop=d == DT - 1).then_inc(nm.added, 1)

        def act_rstd(eng, nm, c, src, ready=None):
            s = BOTH[c]
            eng.wait_ge(*(ready or (nm.summed, c + 1)))
            eng.activation(rstd[:, s], src[:, s], ACT.Ln, bias=eps[:], scale=1.0 / D).then_inc(nm.log, 1)
            eng.wait_ge(nm.log, c + 1)
            eng.activation(rstd[:, s], rstd[:, s], ACT.Exp, scale=-0.5).then_inc(nm.rstd, 1)

        def gain_col(which, d):
            v = V_NORM + which * DT + d
            return gains[:, v:v + 1]

        def dve_scale(eng, nm, which, c, d):
            s = BOTH[c]
            if d == 0:
                eng.wait_ge(nm.rstd, c + 1)
            if d >= 2:
                eng.wait_ge(nm.hi, DT * c + d - 1)
                eng.wait_ge(nm.lo[d % 2], 4 * c + d // 2)
            eng.scalar_tensor_tensor(out=sq_buf[d % 2][:, s], in0=xT[:, d, s], scalar=gain_col(which, d),
                                     in1=rstd[:, s], op0=ALU.mult, op1=ALU.mult).then_inc(nm.scaled, 1)

        def act_h_hi(eng, nm, c, d):
            eng.wait_ge(nm.scaled, DT * c + d + 1)
            eng.activation(h_hi[:, d, BOTH[c]], sq_buf[d % 2][:, BOTH[c]], ACT.Copy).then_inc(nm.hi, 1)

        def h_lo_part(eng, nm, c, d):
            s = BOTH[c]
            eng.wait_ge(nm.hi, DT * c + d + 1)
            eng.tensor_tensor(h_lo[:, d, s], sq_buf[d % 2][:, s], h_hi[:, d, s].bitcast(F32),
                              ALU.subtract).then_inc(nm.lo[d % 2], 1)

        def dve_h_tile(eng, nm, which, c, d):
            dve_scale(eng, nm, which, c, d)
            if d % 2:
                h_lo_part(eng, nm, c, d - 1)

        def act_early_slot(eng, slot, r):
            split_hi_col(eng, slot + r, r, slot > 0, back=4)

        def pool_norm(eng, nm, slot):
            for c in range(2):
                for d in range(1, DT, 2):
                    h_lo_part(eng, nm, c, d)
                split_lo_col(eng, slot + 2 + c, 2 + c)

        def sp_ffn(sp, f):
            wgu = w_gate_up[0, f.which]
            wd = w_down[0, f.which]

            def step(g, first=False):
                cols = [wgu[:, bass.ds(addr(sp, g * 2 * P + c0), P)] for c0 in (0, FF, P, FF + P)]
                rows = [wd[bass.ds(addr(sp, g * 2 * P + j * P), P), :] for j in range(2)]
                for j in range(4):
                    load_col(sp, cols[j], f.slot0 + 4 * g + j, j, not (first and f is ffn_a))
                for j in range(2):
                    if not first:
                        sp.wait_ge(f.rlo, 2 * g + j - 1)
                    elif f is ffn_b and j == 0:
                        sp.wait_ge(m_gated, HEADS)
                    sp.dma_start(row_raw[:, j], rows[j]).then_inc(f.rload[j], 16)

            step(0, True)
            with sp.Fori(1, GROUPS) as g:
                step(g)

        def pe_ffn(pe, f):
            def down(m):
                pe.wait_ge(f.rlo, 2 * m + 2)
                pe.wait_ge(f.alo, 2 * m + 2)
                for d in range(DT):
                    b = (1 + d) % 4
                    if d == 0:
                        pe.wait_ge(f.prod, 2 * m + 1)
                    elif d == 1:
                        pe.wait_ge(f.silu, 2 * m + 2)
                    elif d == 2:
                        pe.wait_ge(f.prod, 2 * m + 2)
                    elif d == 3:
                        pe.wait_ge(f.silu, 2 * m + 3)
                    else:
                        pe.wait_ge(f.xadd, DT * m + d - 3)
                    for t in range(2):
                        mm = pe_three(pe, bank[b], row_hi[:, t, d * P:(d + 1) * P],
                                      row_lo[:, t, d * P:(d + 1) * P], act_hi[:, t], act_lo[:, t],
                                      t == 0, t == 1)
                    mm.then_inc(f.down, 1)

            def last_down():
                m = GROUPS - 1
                pe.wait_ge(f.rlo, 2 * m + 2)
                pe.wait_ge(f.alo, 2 * m + 1)
                pe.wait_ge(f.silu, 2 * m + 2)
                for c in range(2):
                    pe.wait_ge(f.last_alo, c + 1)
                    for d in range(DT):
                        q = DT * c + d
                        if q >= 4:
                            pe.wait_ge(f.xadd, DT * m + q - 3)
                        if (c, d) == (1, 3):
                            pe_norm_sum(pe, f.after, 0, bank[1])
                        for t in range(2):
                            mm = pe_three(pe, bank[(1 + d) % 4], row_hi[:, t, d * P:(d + 1) * P],
                                          row_lo[:, t, d * P:(d + 1) * P], act_hi[:, t], act_lo[:, t],
                                          t == 0, t == 1, (BOTH[c],))
                        mm.then_inc(f.down, 1)

            def step(g, last=False):
                n = f.slot0 + 4 * g
                pe.wait_ge(f.silu, 2 * g - 1)
                pe.wait_ge(f.prod, 2 * g - 1)
                pe_col_unit(pe, n, 0, bank[0])
                down(g - 1)
                for j in (1, 2, 3):
                    pe.wait_ge(f.xadd, DT * (g - 1) + 4 + j)
                    if not last or j < 3:
                        pe_col_unit(pe, n + j, j, bank[j])
                if last:
                    pe.wait_ge(s_clo, n + 4)
                    for c in range(2):
                        for k in range(DT):
                            mm = pe_col_tile(pe, 3, k, bank[3], (BOTH[c],))
                        mm.then_inc(s_cdone if c else f.last_up, 1)

            pe_first_units(pe, f.slot0, f.norm, rows_as_cols, DT - 1 if f is ffn_a else 4)
            for j in (2, 3):
                pe_col_unit(pe, f.slot0 + j, j, bank[j])
            with pe.Fori(1, GROUPS - 1) as g:
                step(g)
            step(GROUPS - 1, last=True)
            last_down()

        def act_ffn(act, f):
            def silu(g, t):
                act.wait_ge(s_cdone, f.slot0 + 4 * g + 2 * t + 1)
                if not (isinstance(g, int) and g == 0 and t == 0):
                    act.wait_ge(f.prod, 2 * g + t)
                act.activation(silu_g[:], bank[2 * t][:], ACT.Silu).then_inc(f.silu, 1)

            def hidden_hi(g, t):
                act.wait_ge(f.prod, 2 * g + t + 1)
                act.activation(act_hi[:, t], prod[:], ACT.Copy).then_inc(f.ahi, 1)

            def step(g, first=False, last=False):
                n = f.slot0 + 4 * g
                if not first:
                    split_hi_col(act, n + 1, 1)
                silu(g, 0)
                if not first:
                    split_hi_col(act, n + 2, 2)
                if first:
                    act.wait_ge(s_cdone, f.slot0 + 2)
                else:
                    act.wait_ge(f.down, DT * g)
                for t in range(2):
                    act.wait_ge(f.rload[t], 16 * g + 16)
                    act.activation(row_hi[:, t], row_raw[:, t], ACT.Copy).then_inc(f.rhi, 1)
                hidden_hi(g, 0)
                if not first:
                    split_hi_col(act, n + 3, 3)
                silu(g, 1)
                if not last:
                    split_hi_col(act, n + 4, 0)
                    hidden_hi(g, 1)
                else:
                    for c, s in enumerate(BOTH):
                        act.wait_ge(f.last_prod, c + 1)
                        act.activation(act_hi[:, 1, s], prod[:, s], ACT.Copy).then_inc(f.last_ahi, 1)

            step(0, True)
            with act.Fori(1, GROUPS - 1) as g:
                step(g)
            step(GROUPS - 1, last=True)

        DVE_SCALES = (4, 5)

        def act_norm_after(act, nm, ready, base, slot):
            hi = slot is not None
            act.preload_act_table_set(LN_EXP)
            if hi:
                split_hi_col(act, slot, 0, False, mix_first[0])
            for d in range(DT):
                act_square(act, nm, 0, d, ready, base + d + 1)
                if hi and d == 2:
                    split_hi_col(act, slot + 1, 1, False, mix_first[0])
            for d in range(DT):
                act_square(act, nm, 1, d, ready, base + DT + d + 1)
                if d == 3:
                    act_rstd(act, nm, 0, bank[1])
                if hi and d >= 4:
                    act_h_hi(act, nm, 0, d - 4)
                elif not hi and 2 <= d < 2 + DT - DVE_SCALES[0]:
                    act_gain(act, 0, DVE_SCALES[0] + d - 2)
            if not hi:
                for d in range(DVE_SCALES[1], DT):
                    act_gain(act, 1, d)
            if hi:
                for d in range(4, 6):
                    act_h_hi(act, nm, 0, d)
            act_rstd(act, nm, 1, bank[2])
            if hi:
                for d in range(6, DT):
                    act_h_hi(act, nm, 0, d)
                act_early_slot(act, slot, 2)
                for d in range(DT):
                    act_h_hi(act, nm, 1, d)
                act_early_slot(act, slot, 3)

        def pool_ffn(pool, f):
            def step(g, first=False, last=False):
                n = f.slot0 + 4 * g
                if not first:
                    split_lo_col(pool, n + 1, 1)
                    split_lo_col(pool, n + 2, 2)
                for t in range(2):
                    pool.wait_ge(f.rhi, 2 * g + t + 1)
                    pool.tensor_tensor(row_lo[:, t], row_raw[:, t], row_hi[:, t].bitcast(F32),
                                       ALU.subtract).then_inc(f.rlo, 1)
                if not first:
                    split_lo_col(pool, n + 3, 3)
                if not last:
                    split_lo_col(pool, n + 4, 0)

            step(0, True)
            with pool.Fori(1, GROUPS - 1) as g:
                step(g)
            step(GROUPS - 1, last=True)

        def dve_ffn(dve, f, scale):
            def down(m):
                for d in range(DT):
                    dve.wait_ge(f.down, DT * m + d + 1)
                    dve.scalar_tensor_tensor(out=xT[:, d], in0=bank[(1 + d) % 4][:], scalar=0.5,
                                             in1=xT[:, d], op0=ALU.mult, op1=ALU.add).then_inc(f.xadd, 1)

            def last_down():
                for c in range(2):
                    s = BOTH[c]
                    for d in range(DT):
                        dve.wait_ge(f.down, DT * (GROUPS - 1) + DT * c + d + 1)
                        dve.scalar_tensor_tensor(out=xT[:, d, s], in0=bank[(1 + d) % 4][:, s], scalar=0.5,
                                                 in1=xT[:, d, s], op0=ALU.mult, op1=ALU.add).then_inc(f.xadd, 1)
                        if d:
                            dve_add_square(dve, f.after, c, d - 1)
                        if c == 1 and d >= 4:
                            scale(0, d - 4)
                    dve_add_square(dve, f.after, c, DT - 1)
                for d in range(4, DT):
                    scale(0, d)
                for d in range(DT):
                    scale(1, d)

            def step(g, first=False, last=False):
                if not first:
                    down(g - 1)
                for t in range(1 if last else 2):
                    if first and t == 0:
                        dve.wait_ge(f.norm.lo[1], DT)
                    else:
                        dve.wait_ge(f.alo, 2 * g + t)
                    dve.wait_ge(f.silu, 2 * g + t + 1)
                    dve.wait_ge(s_cdone, f.slot0 + 4 * g + 2 * t + 2)
                    dve.tensor_tensor(prod[:], silu_g[:], bank[2 * t + 1][:], ALU.mult).then_inc(f.prod, 1)
                    dve.wait_ge(f.ahi, 2 * g + t + 1)
                    dve.tensor_tensor(act_lo[:, t], prod[:], act_hi[:, t].bitcast(F32),
                                      ALU.subtract).then_inc(f.alo, 1)

            def last_hidden():
                dve.wait_ge(f.alo, 2 * GROUPS - 1)
                dve.wait_ge(f.silu, 2 * GROUPS)
                for c, s in enumerate(BOTH):
                    if c == 0:
                        dve.wait_ge(f.last_up, 1)
                    else:
                        dve.wait_ge(s_cdone, f.slot0 + 4 * GROUPS)
                    dve.tensor_tensor(prod[:, s], silu_g[:, s], bank[3][:, s], ALU.mult).then_inc(f.last_prod, 1)
                    dve.wait_ge(f.last_ahi, c + 1)
                    dve.tensor_tensor(act_lo[:, 1, s], prod[:, s], act_hi[:, 1, s].bitcast(F32),
                                      ALU.subtract).then_inc(f.last_alo, 1)

            step(0, True)
            with dve.Fori(1, GROUPS - 1) as g:
                step(g)
            step(GROUPS - 1, last=True)
            last_hidden()
            last_down()

        small = bank[2]

        def round_bank(n):
            return {3: bank[0], 5: bank[0], 7: bank[3]}.get(n, small)

        def key_blocks(ap, b):
            return ap.rearrange("p (a j x) -> p a j x", j=4, x=b)[:, :, 0:3, :]

        def queries_after(ap, b, j):
            return ap.rearrange("p c (a y) -> p c a y", y=4 * b)[:, :, :, (j + 1) * b:4 * b]

        def by_tile(ap):
            return ap.rearrange("p (c t) -> p c t", t=P)

        def query_place(n, j):
            tiles = work[:, n % 2, T:T + Q_ALL].rearrange("p (c w) -> p c w", w=QW)
            return tiles[:, :, Q_OFF[j]:Q_OFF[j] + Q_LEN[j]].rearrange("p c (a y) -> p c a y", y=(3 - j) * ROUNDS[n])

        def sp_mixer(sp):
            def step(i):
                cols = [w_in[0][:, bass.ds(addr(sp, i * P + c0), P)] for c0 in (D, 0, 2 * D, 3 * D)]
                for j in range(4):
                    load_col(sp, cols[j], MIX0 + 4 * i + j, j, alone=True)

            step(0)
            sp.wait_ge(ffn_a.xadd, DT * (GROUPS + 1))
            sp.dma_start(x_park, xT[:].rearrange("p d t -> p (d t)")).then_inc(s_park, 16)
            with sp.Fori(1, HEADS) as i:
                step(i)

        def pe_mixer(pe):
            def updates(h):
                pe.wait_ge(m_knat, 2 * h + 2)
                pe.wait_ge(m_vnat, 2 * h + 2)
                pe.wait_ge(m_sel, SEL * (h + 1))
                for c in range(NC - 1):
                    mm = pe.matmul(small[:, c * P:(c + 1) * P], k_nat[:, c], v_nat[:, c],
                                   start=True, stop=True)
                mm.then_inc(m_upd, 1)

            def outputs(h):
                pe.wait_ge(m_qcum, h + 1)
                pe.wait_ge(m_state, 7 * h + 7)
                for c in range(NC):
                    s = slice(c * P, (c + 1) * P)
                    mm = pe.matmul(bank[3][:, s], v_nat[:, c], scores[:, s], start=True, stop=c == 0)
                    if c:
                        mm = pe.matmul(bank[3][:, s], state[:, c], q_cum[:, s], start=False, stop=True)
                mm.then_inc(m_o, 1)

            def head_sum(h):
                pe.wait_ge(m_osq_lo, h + 1)
                for s in BOTH:
                    pe.matmul(small[:, s], ones_r[:], osq_hi[:, s], start=True, stop=False)
                for s in BOTH:
                    mm = pe.matmul(small[:, s], ones_r[:], osq_lo[:, s], start=False, stop=True)
                mm.then_inc(m_osum, 1)

            def score(i, n, first=False):
                r, half = n // 2, n % 2
                if half == 0:
                    pe.wait_ge(m_ops, OPS * i + r + 1)
                if n in (1, 2):
                    pe.wait_ge(m_sel, SEL * i + 3 * n)
                elif n == 3:
                    pe.wait_ge(m_vt, i + 1)
                elif n > 3:
                    pe.wait_ge(m_sel, SEL * i + 3 * (n - 1))
                elif not first:
                    pe.wait_ge(m_hlog, i)
                for c in range(4):
                    t = 4 * half + c
                    mm = pe.matmul(round_bank(n)[:, c * PW:c * PW + QW], work[:, r % 2, t * P:(t + 1) * P],
                                   work[:, r % 2, T + t * QW:T + (t + 1) * QW], start=True, stop=True)
                mm.then_inc(m_lvl, 1)

            def turn_keys(h, half):
                if half == 0:
                    pe.wait_ge(m_ops, OPS * (h + 1))
                    pe.wait_ge(m_sel, SEL * h + 6 * NR + 2)
                turn(k_end, half, small[:, BOTH[half]], m_kturn)

            def last_round(i, half):
                n = 2 * NR + half
                if half == 0:
                    pe.wait_ge(m_ops, OPS * i + NR + 1)
                    pe.wait_ge(m_sel, SEL * i + 3 * (n - 1))
                else:
                    pe.wait_ge(m_vnat, 2 * i + 2)
                for c in range(4):
                    t = 4 * half + c
                    mm = pe.matmul(round_bank(n)[:, c * PW:c * PW + QW], k_t[:, t * P:(t + 1) * P],
                                   q_all[:, t], start=True, stop=True)
                mm.then_inc(m_lvl, 1)

            def turn(src, half, place, done):
                for c in range(4):
                    mm = pe.transpose(place[:, c * P:(c + 1) * P],
                                      src[:, half * HALF + c * P:half * HALF + (c + 1) * P], ident[:])
                mm.then_inc(done, 1)

            def step(i, first=False):
                n = MIX0 + 4 * i
                if first:
                    pe_first_units(pe, n, norms[1], mix_first)
                else:
                    pe.wait_ge(m_sel, SEL * (i - 1) + 6 * NR)
                    pe_col_unit(pe, n, 0, bank[0], between=lambda k: turn_keys(i - 1, k // 2) if k in (1, 3) else None)
                    updates(i - 1)
                    pe.wait_ge(m_og, i)
                    pe_col_unit(pe, n + 1, 1, bank[1])
                    outputs(i - 1)

                def in_v(k):
                    if k == 3:
                        head_sum(i - 1)
                    if k == 5:
                        score(i, 0)
                    if k == 7:
                        score(i, 1)

                def in_g(k):
                    if k % 2 and not first:
                        score(i, 2 + k // 2)
                    elif k in (3, 5, 7) and first:
                        score(i, (k - 3) // 2, k == 3)

                if first:
                    pe_col_unit(pe, n + 2, 2, bank[3])
                else:
                    pe.wait_ge(m_sigf, i + 1)
                    pe_col_unit(pe, n + 2, 2, bank[0], between=in_v)
                pe.wait_ge(m_q, i + 1)
                pe_col_unit(pe, n + 3, 3, bank[1], between=in_g)
                pe.wait_ge(m_vt, i + 1)
                if not first:
                    pe.wait_ge(m_norm, i)
                if first:
                    score(i, 3)
                turn(v_t, 0, bank[3][:, LO], m_vturn)
                turn(v_t, 1, bank[3][:, UP], m_vturn)
                if first:
                    score(i, 4)
                    score(i, 5)
                last_round(i, 0)
                last_round(i, 1)

            step(0, True)
            with pe.Fori(1, HEADS) as i:
                step(i)

            def out_tiles(u, heads):
                for k in heads:
                    if u == 0:
                        wait_gated(pe, k)
                    mm = pe_col_tile(pe, u, k, bank[u])
                if k == DT - 1:
                    mm.then_inc(s_cdone, 1)

            turn_keys(HEADS - 1, 0)
            turn_keys(HEADS - 1, 1)
            pe.wait_ge(s_clo, OUT0 + 1)
            pe.wait_ge(m_sel, SEL * (HEADS - 1) + 6 * NR)
            out_tiles(0, (0,))
            updates(HEADS - 1)
            out_tiles(0, (1, 2))
            outputs(HEADS - 1)
            out_tiles(0, range(3, 5))
            head_sum(HEADS - 1)
            out_tiles(0, range(5, DT - 1))
            pe.wait_ge(s_clo, OUT0 + 2)
            pe.wait_ge(m_og, HEADS)
            out_tiles(1, range(0, DT - 2))
            out_tiles(0, (DT - 1,))
            out_tiles(1, (DT - 2, DT - 1))

        def act_mixer(act):
            def exp(i, n):
                act.wait_ge(m_dif, OPS * i + n + 1)
                if n < NR:
                    keys = work[:, n % 2, 0:T].rearrange("p (a y) -> p a y", y=4 * ROUNDS[n])[:, :, 0:3 * ROUNDS[n]]
                    act.activation(keys, keys, ACT.Exp)
                    part = work[:, n % 2, T:T + Q_ALL]
                elif n == NR:
                    part = work[:, 1, T:T + HALF]
                else:
                    part = work[:, 1, 0:T]
                act.activation(part, part, ACT.Exp).then_inc(m_exp, 1)

            def o_square(h):
                act.wait_ge(m_o, h + 1)
                act.activation(logf[:], bank[3][:], ACT.Square).then_inc(m_osq, 1)
                act.wait_ge(m_osq, h + 1)
                act.activation(osq_hi[:], logf[:], ACT.Copy).then_inc(m_osq_hi, 1)

            def sigmoid_q(i):
                act.wait_ge(s_cdone, MIX0 + 4 * i + 2)
                act.activation(sig_q[:], bank[1][:], ACT.Sigmoid).then_inc(m_sigq, 1)

            def key_rows(h):
                for half in range(2):
                    act.wait_ge(m_kturn, 2 * h + half + 1)
                    act.activation(k_nat[:, 4 * half:4 * half + 4],
                                   small[:, BOTH[half]].rearrange("p (c v) -> p c v", v=P),
                                   ACT.Copy).then_inc(m_knat, 1)

            def head_rstd(h):
                act.wait_ge(m_osum, h + 1)
                act.activation(sig_q[:], small[:], ACT.Ln, bias=eps[:], scale=1.0 / HD).then_inc(m_hlog, 1)
                act.wait_ge(m_hlog, h + 1)
                act.activation(sig_q[:], sig_q[:], ACT.Exp, scale=-0.5).then_inc(m_hrstd, 1)

            def step(i, first=False):
                n = MIX0 + 4 * i
                if not first:
                    split_hi_col(act, n + 1, 1)
                    key_rows(i - 1)
                act.wait_ge(s_cdone, n + 1)
                if not first:
                    act.wait_ge(m_og, i)
                act.activation(sig_a[:], bank[0][:], ACT.Sigmoid).then_inc(m_sigf, 1)
                if first:
                    sigmoid_q(i)
                act.preload_act_table_set(LN_EXP)
                act.wait_ge(m_sigf, i + 1)
                act.activation(logf[:], sig_a[:], ACT.Ln, bias=lbv[:, L_LB, bass.ds(i, 1)],
                               scale=lbv[:, L_ONE_MINUS, bass.ds(i, 1)]).then_inc(m_logf, 1)
                if not first:
                    split_hi_col(act, n + 2, 2)
                act.wait_ge(m_cum, i + 1)
                if not first:
                    act.wait_ge(m_state, 7 * i)
                act.activation(tile_dec[:], cum[:, P - 1:T:P], ACT.Exp).then_inc(m_tdec, 1)
                if not first:
                    sigmoid_q(i)
                    act.preload_act_table_set(LN_EXP)
                exp(i, 0)
                if not first:
                    o_square(i - 1)
                exp(i, 1)
                if not first:
                    split_hi_col(act, n + 3, 3)
                act.activation(q_cum[:], cum[:], ACT.Exp).then_inc(m_qexp, 1)
                if not first:
                    act.wait_ge(m_q, i + 1)
                    head_rstd(i - 1)
                act.wait_ge(s_cdone, n + 3)
                act.activation(v_t[:], bank[3 if first else 0][:], ACT.Copy).then_inc(m_vt, 1)
                split_hi_col(act, n + 4, 0)
                for m in (2, 3, 4):
                    exp(i, m)
                act.wait_ge(s_cdone, n + 4)
                act.wait_ge(m_k, i + 1)
                act.activation(sig_a[:], bank[1][:], ACT.Sigmoid).then_inc(m_sigg, 1)
                for half in range(2):
                    act.wait_ge(m_vturn, 2 * i + half + 1)
                    act.activation(v_nat[:, 4 * half:4 * half + 4],
                                   bank[3][:, BOTH[half]].rearrange("p (c v) -> p c v", v=P),
                                   ACT.Copy).then_inc(m_vnat, 1)

            step(0, True)
            with act.Fori(1, HEADS) as i:
                step(i)
            act.wait_ge(s_cdone, OUT0)
            for h in range(HEADS - 1):
                if h == 2:
                    key_rows(HEADS - 1)
                    act.preload_act_table_set(LN_EXP)
                    split_hi_col(act, OUT0 + 1, 1)
                act.wait_ge(m_gated, h + 1)
                act.activation(h_hi[:, h], og[:, h], ACT.Copy).then_inc(g_hi, 1)
                if h == 4:
                    o_square(HEADS - 1)
            head_rstd(HEADS - 1)
            act.wait_ge(m_gated, HEADS)
            act.activation(h_hi[:, HEADS - 1], og[:, HEADS - 1], ACT.Copy).then_inc(g_hi, 1)

        def pool_mixer(pool):
            def exponents(i, n):
                if n < 2:
                    if not (isinstance(i, int) and i == 0):
                        pool.wait_ge(m_lvl, HALVES * i - 2)
                        pool.wait_ge(m_ops, OPS * i)
                elif n == 2:
                    pool.wait_ge(m_lvl, HALVES * i + 2)
                else:
                    pool.wait_ge(m_lvl, HALVES * i + 4)
                if n == NR:
                    pairs = cum[:].rearrange("p (a two) -> p a two", two=2)
                    pool.tensor_tensor(work[:, 1, T:T + HALF].rearrange("p (a o) -> p a o", o=1),
                                       pairs[:, :, 1:2], pairs[:, :, 0:1], ALU.subtract).then_inc(m_dif, 1)
                    return
                if n > NR:
                    c3 = cum[:].rearrange("p (c t) -> p c t", t=P)
                    pool.tensor_tensor(work[:, 1, 0:T].rearrange("p (c t) -> p c t", t=P),
                                       c3[:, :, P - 1:P].broadcast_to([P, NC, P]), c3,
                                       ALU.subtract).then_inc(m_dif, 1)
                    return
                b = ROUNDS[n]
                c4 = key_blocks(cum[:], b)
                pool.tensor_tensor(key_blocks(work[:, n % 2, 0:T], b),
                                   c4[:, :, :, b - 1:b].broadcast_to([P, T // (4 * b), 3, b]), c4, ALU.subtract)
                for j in range(3):
                    after = queries_after(by_tile(cum[:]), b, j)
                    groups = cum[:].rearrange("p (c a y) -> p c a y", c=NC, y=4 * b)
                    ref = groups[:, :, :, (j + 1) * b - 1:(j + 1) * b]
                    op = pool.tensor_tensor(query_place(n, j), after,
                                            ref.broadcast_to([P, NC, P // (4 * b), (3 - j) * b]), ALU.subtract)
                op.then_inc(m_dif, 1)

            def step(i, first=False):
                n = MIX0 + 4 * i
                if not first:
                    split_lo_col(pool, n + 1, 1)
                    split_lo_col(pool, n + 2, 2)
                pool.wait_ge(m_cum, i + 1)
                exponents(i, 0)
                exponents(i, 1)
                if not first:
                    split_lo_col(pool, n + 3, 3)
                exponents(i, 2)
                split_lo_col(pool, n + 4, 0)
                exponents(i, 3)
                exponents(i, 4)

            step(0, True)
            with pool.Fori(1, HEADS) as i:
                step(i)
            gated_lo(pool, 0, g_lo_first)
            split_lo_col(pool, OUT0 + 1, 1)

        def wait_gated(eng, h):
            if h == 0:
                eng.wait_ge(g_lo_first, 1)
            else:
                eng.wait_ge(g_lo, h)

        def gated_lo(eng, h, done):
            eng.wait_ge(g_hi, h + 1)
            eng.tensor_tensor(h_lo[:, h], og[:, h], h_hi[:, h].bitcast(F32), ALU.subtract).then_inc(done, 1)

        def dve_mixer(dve):
            def state_chain(h):
                dve.wait_ge(m_upd, h + 1)
                dve.wait_ge(m_tdec, h + 1)
                dve.tensor_copy(state[:, 1], small[:, 0:P]).then_inc(m_state, 1)
                for c in range(1, NC - 1):
                    dve.wait_ge(m_state, 7 * h + c)
                    dve.scalar_tensor_tensor(out=state[:, c + 1], in0=state[:, c],
                                             scalar=tile_dec[:, c:c + 1],
                                             in1=small[:, c * P:(c + 1) * P],
                                             op0=ALU.mult, op1=ALU.add).then_inc(m_state, 1)

            def square_lo(h):
                dve.wait_ge(m_osq_hi, h + 1)
                dve.tensor_tensor(osq_lo[:], logf[:], osq_hi[:].bitcast(F32), ALU.subtract).then_inc(m_osq_lo, 1)

            def gate(h):
                dve.wait_ge(m_hrstd, h + 1)
                dve.scalar_tensor_tensor(out=sig_q[:], in0=bank[3][:],
                                         scalar=gains[:, V_HEAD:V_HEAD + 1], in1=sig_q[:],
                                         op0=ALU.mult, op1=ALU.mult).then_inc(m_norm, 1)
                dve.wait_ge(m_og, h + 1)
                dve.wait_ge(m_norm, h + 1)
                dve.tensor_tensor(og[:, bass.ds(h, 1)], og[:, bass.ds(h, 1)],
                                  sig_q[:].rearrange("p (o t) -> p o t", o=1),
                                  ALU.mult).then_inc(m_gated, 1)

            def operands(i, n):
                dve.wait_ge(m_exp, OPS * i + n + 1)
                if n == NR:
                    dve.tensor_tensor(q_all[:, :, P:QW].rearrange("p c (a o) -> p c a o", o=1),
                                      q_all[:, :, 0:P].rearrange("p c (a two) -> p c a two", two=2)[:, :, :, 1:2],
                                      work[:, 1, T:T + HALF].rearrange("p (c a o) -> p c a o", c=NC, o=1),
                                      ALU.mult).then_inc(m_ops, 1)
                    return
                if n > NR:
                    dve.tensor_tensor(k_end[:], k_t[:], work[:, 1, 0:T], ALU.mult).then_inc(m_ops, 1)
                    return
                b = ROUNDS[n]
                here = key_blocks(work[:, n % 2, 0:T], b)
                dve.tensor_tensor(here, key_blocks(k_t[:], b), here, ALU.mult)
                for j in range(3):
                    here = query_place(n, j)
                    op = dve.tensor_tensor(here, queries_after(q_all[:, :, 0:P], b, j), here, ALU.mult)
                op.then_inc(m_ops, 1)

            def select(i, n):
                r, half = n // 2, n % 2
                tokens = scores[:, half * HALF:(half + 1) * HALF]
                done = 3 * n - max(n - 2 * NR, 0)
                for j in range(3 if r < NR else 2):
                    if not (isinstance(i, int) and i == 0 and done + j == 0):
                        dve.wait_ge(m_sel, SEL * i + done + j)
                    if j == 0:
                        dve.wait_ge(m_lvl, HALVES * i + n + 1)
                    dve.sem_inc(m_seen, 1)
                    tiles = round_bank(n)[:].rearrange("p (c w) -> p c w", w=PW)
                    if r < NR:
                        b = ROUNDS[r]
                        shape = [P, 4, P // (4 * b), (3 - j) * b]
                        place = queries_after(by_tile(tokens), b, j)
                        mask = masks[:, M_OFF[r]:M_OFF[r + 1]].bitcast(U32).rearrange(
                            "p (o a j) -> p o a j", o=1, j=4)[:, :, :, j:j + 1].broadcast_to(shape)
                        src = tiles[:, :, Q_OFF[j]:Q_OFF[j] + Q_LEN[j]].rearrange(
                            "p c (a y) -> p c a y", y=(3 - j) * b)
                    elif j == 0:
                        place = by_tile(tokens)
                        mask = ident[:].bitcast(U32).rearrange("p (o t) -> p o t", o=1).broadcast_to([P, 4, P])
                        src = tiles[:, :, 0:P]
                    else:
                        place = tokens.rearrange("p (c a two) -> p c a two", c=4, two=2)[:, :, :, 1:2]
                        mask = masks[:, M_OFF[NR]:M_OFF[NR + 1]].bitcast(U32).rearrange(
                            "p (o a x) -> p o a x", o=1, x=1).broadcast_to([P, 4, 64, 1])
                        src = tiles[:, :, P:QW].rearrange("p c (a x) -> p c a x", x=1)
                    dve.copy_predicated(place, mask, src).then_inc(m_sel, 1)

            def step(i, first=False):
                n = MIX0 + 4 * i
                if not first:
                    dve.wait_ge(m_kturn, 2 * i)
                dve.wait_ge(m_sigf, i + 1)
                dve.tensor_scalar(k_t[:], sig_a[:], lbv[:, L_MINUS, bass.ds(i, 1)],
                                  lbv[:, L_ONE_MINUS, bass.ds(i, 1)], ALU.mult, ALU.add).then_inc(m_k, 1)
                if not first:
                    state_chain(i - 1)
                dve.wait_ge(m_logf, i + 1)
                for c in range(NC):
                    s = slice(c * P, (c + 1) * P)
                    cs = dve.tensor_tensor_scan(cum[:, s], ones[:], logf[:, s], 0.0, ALU.mult, ALU.add)
                cs.then_inc(m_cum, 1)
                dve.wait_ge(m_sigq, i + 1)
                dve.scalar_tensor_tensor(out=q_all[:, :, 0:P], in0=by_tile(sig_q[:]), scalar=QSCALE, in1=by_tile(bank[1][:]),
                                         op0=ALU.mult, op1=ALU.mult).then_inc(m_q, 1)
                dve.wait_ge(m_q, i + 1)
                if not first:
                    square_lo(i - 1)
                operands(i, 0)
                if first:
                    select(i, 0)
                    operands(i, 1)
                else:
                    operands(i, 1)
                    select(i, 0)
                select(i, 1)
                if not first:
                    gate(i - 1)
                select(i, 2)
                operands(i, 2)
                select(i, 3)
                operands(i, 3)
                select(i, 4)
                operands(i, 4)
                select(i, 5)
                for m in (6, 7):
                    select(i, m)
                dve.wait_ge(m_qexp, i + 1)
                dve.tensor_tensor(by_tile(q_cum[:]), by_tile(q_cum[:]), q_all[:, :, 0:P], ALU.mult).then_inc(m_qcum, 1)
                dve.wait_ge(m_sigg, i + 1)
                if first:
                    dve.wait_ge(s_park, 16)
                dve.tensor_tensor(og[:, bass.ds(i, 1)], sig_a[:].rearrange("p (o t) -> p o t", o=1),
                                  bank[1][:].rearrange("p (o t) -> p o t", o=1),
                                  ALU.mult).then_inc(m_og, 1)

            for done in norms[1].lo:
                dve.wait_ge(done, DT)
            dve.memset(scores[:], 0.0).then_inc(m_zero, 1)
            dve.memset(work[:, :, 0:T], 0.0).then_inc(m_zero, 1)
            dve.wait_ge(m_zero, 2)
            step(0, True)
            with dve.Fori(1, HEADS) as i:
                step(i)
            for h in range(1, 4):
                gated_lo(dve, h, g_lo)
            state_chain(HEADS - 1)
            gated_lo(dve, 4, g_lo)
            square_lo(HEADS - 1)
            for h in range(5, HEADS - 1):
                gated_lo(dve, h, g_lo)
            gate(HEADS - 1)
            gated_lo(dve, HEADS - 1, g_lo)

        def act_out(act, nm):
            for d in range(DT - 2):
                split_hi_col(act, OUT0 + d + 2, (d + 2) % 4)
                act_square(act, nm, 0, d, o_add, d + 1)
            act_square(act, nm, 0, 6, o_add, 7)
            act_square(act, nm, 0, 7, o_add, 8)
            for d in range(DT - 2):
                act_square(act, nm, 1, d)
            for n in (FFN0, FFN0 + 1):
                split_hi_col(act, n, n % 4, False, rows_as_cols[0])
            act_rstd(act, nm, 0, bank[1])
            for d in range(4):
                act_h_hi(act, nm, 0, d)
            act_square(act, nm, 1, 6, o_add, 9)
            for d in (4, 5):
                act_h_hi(act, nm, 0, d)
            act_square(act, nm, 1, 7, o_add, 10)
            for d in (6, 7):
                act_h_hi(act, nm, 0, d)
            act_early_slot(act, FFN0, 2)
            act_rstd(act, nm, 1, bank[2])
            for d in range(DT):
                act_h_hi(act, nm, 1, d)
            act_early_slot(act, FFN0, 3)

        def dve_out(dve, nm, which):
            def x_add(d, s):
                dve.tensor_tensor(xT[:, d, s], xT[:, d, s], bank[d % 4][:, s], ALU.add).then_inc(o_add, 1)

            for d in range(DT - 2):
                dve.wait_ge(s_cdone, OUT0 + d + 1)
                dve.wait_ge(s_back[d], 16)
                x_add(d, slice(0, T))
                if d:
                    dve_add_square(dve, nm, 0, d - 1)
            for u, d in enumerate((DT - 2, DT - 1)):
                dve.wait_ge(o_last, u + 1)
                dve.wait_ge(s_back[d], 16)
                x_add(d, BOTH[0])
                dve_add_square(dve, nm, 0, d - 1)
            dve_add_square(dve, nm, 0, DT - 1)
            for d in range(DT - 2):
                dve_add_square(dve, nm, 1, d)
            for d in range(4):
                dve_h_tile(dve, nm, which, 0, d)
            for d, turns in ((DT - 2, (4, 5)), (DT - 1, (6, 7))):
                dve.wait_ge(s_cdone, OUT0 + d + 1)
                x_add(d, BOTH[1])
                dve_add_square(dve, nm, 1, d)
                for t in turns:
                    dve_h_tile(dve, nm, which, 0, t)
            for d in range(DT):
                dve_h_tile(dve, nm, which, 1, d)

        def act_gain(eng, c, d):
            s = BOTH[c]
            eng.activation(xT[:, d, s], xT[:, d, s], ACT.Copy,
                           scale=gains[:, V_FINAL + d:V_FINAL + d + 1]).then_inc(s_gained, 1)

        def pool_final(eng):
            done = 0
            for c in range(2):
                for d in range(DVE_SCALES[c], DT):
                    done += 1
                    eng.wait_ge(norms[3].rstd, c + 1)
                    eng.wait_ge(s_gained, done)
                    eng.tensor_tensor(xT[:, d, BOTH[c]], xT[:, d, BOTH[c]], rstd[:, BOTH[c]],
                                      ALU.mult).then_inc(s_final[1], 1)

        DVE_PLACES = (4, 6)
        ACT_PLACES = (0, 1, 2, 3, 5, 7)

        def wait_placed(eng, t):
            who = 0 if t in DVE_PLACES else 1
            eng.wait_ge(s_placed_out[who], (DVE_PLACES, ACT_PLACES)[who].index(t) + 1)

        @block.sync
        def _(sp):
            for t in range(NC):
                if t == 4:
                    sp.dma_start(vec_rows[V_NORM:V_FINAL], norm_gains[0].rearrange("w (a p) -> (w a) p", p=P)).then_inc(s_vec, 16)
                    sp.dma_start(vec_rows[V_FINAL:V_LOGIT0], final_gain.rearrange("(a p) -> a p", p=P)).then_inc(s_vec, 16)
                    sp.dma_start(vec_rows[V_LOGIT0:V_HEAD], lb_logits.rearrange("w (a p) -> (w a) p", p=P)).then_inc(s_vec, 16)
                    sp.dma_start(vec_rows[V_HEAD:NVEC], head_gain).then_inc(s_vec, 16)
                if t >= 4:
                    sp.wait_ge(s_turned, t - 3)
                sp.dma_start(stage[:, t % 4], x[0, t * P:(t + 1) * P, :]).then_inc(s_xload[t % 4], 16)
            sp_ffn(sp, ffn_a)
            sp_mixer(sp)
            sp.wait_ge(s_park, 16)
            for d in range(4):
                load_col(sp, w_out[0][:, d * P:(d + 1) * P], OUT0 + d, d)
            for d in range(DT):
                wait_gated(sp, d)
                sp.dma_start(xT[:, d], x_park[:, d * T:(d + 1) * T]).then_inc(s_back[d], 16)
            for d in range(4, DT):
                load_col(sp, w_out[0][:, d * P:(d + 1) * P], OUT0 + d, d % 4)
            sp_ffn(sp, ffn_b)
            for t in range(NC):
                wait_placed(sp, t)
                sp.dma_start(out[0, t * P:(t + 1) * P, :], stage[:, t % 4]).then_inc(s_out[t % 4], 16)
            for done in s_out:
                sp.wait_ge(done, 16 * NC // 4)

        @block.gpsimd
        def _(pool):
            pool.memset(ones[:], 1.0).then_inc(s_ones, 1)
            pool.memset(eps[:], EPS).then_inc(s_eps, 1)
            pool.memset(ident[:], 0.0).then_inc(s_ident, 1)
            pool.memset(masks[:], 1.0).then_inc(s_mask, 1)
            pool.wait_ge(s_ident, 1)
            pool.affine_select(out=ident[:], in_=ident[:], compare_op=ALU.not_equal, fill=1.0, base=0,
                               pattern=[[-1, P]], channel_multiplier=1).then_inc(s_ident, 1)
            for n, (b, step) in enumerate(MASKS):
                m = masks[:, M_OFF[n]:M_OFF[n + 1]]
                pool.wait_ge(s_mask, 2 * n + 1)
                pool.affine_select(out=m, in_=m, compare_op=ALU.is_ge, fill=0.0, base=0,
                                   pattern=[[-step, P // step]], channel_multiplier=1).then_inc(s_mask, 1)
                pool.wait_ge(s_mask, 2 * n + 2)
                pool.affine_select(out=m, in_=m, compare_op=ALU.is_ge, fill=0.0, base=b - 1,
                                   pattern=[[step, P // step]], channel_multiplier=-1).then_inc(s_mask, 1)
            for n in range(2):
                split_lo_col(pool, n, n, *rows_as_cols)
            pool_norm(pool, norms[0], 0)
            pool_ffn(pool, ffn_a)
            for n in (MIX0, MIX0 + 1):
                split_lo_col(pool, n, n % 4, *mix_first)
            pool_norm(pool, norms[1], MIX0)
            pool_mixer(pool)
            for n in range(OUT0 + 2, FFN0):
                split_lo_col(pool, n, n % 4)
            for n in (FFN0, FFN0 + 1):
                split_lo_col(pool, n, n % 4, *rows_as_cols)
            pool_norm(pool, norms[2], FFN0)
            pool_ffn(pool, ffn_b)
            pool_final(pool)

        @block.scalar
        def _(act):
            act.preload_act_table_set(LN_EXP)
            act.wait_ge(s_ones, 1)
            act.activation(ones_r[:], ones[:], ACT.Copy).then_inc(s_ones, 1)

            def place(t):
                act.wait_ge(s_turned, t + 1)
                act.activation(xT[:, :, t * P:(t + 1) * P], bank[1][:].rearrange("p (d t) -> p d t", t=P),
                               ACT.Copy).then_inc(s_placed[1], 1)

            place(1)
            place(3)
            act.wait_ge(s_placed[0], NC // 4)
            act.wait_ge(s_placed[1], NC // 4)
            for d in range(DT):
                act_square(act, norms[0], 0, d)
                if d == 1:
                    place(5)
                if d == 4:
                    place(7)
                    act.wait_ge(s_lb, 3)
                    act.activation(lbv[:, L_E0:L_E1 + 1], lbv[:, L_E0:L_E1 + 1], ACT.Exp).then_inc(s_lbexp, 1)
            for n in range(2):
                split_hi_col(act, n, n, False, rows_as_cols[0])
            act.wait_ge(s_eps, 1)
            act_rstd(act, norms[0], 0, bank[2], (norms[0].added, DT))
            act.wait_ge(s_placed[0], NC // 2)
            act.wait_ge(s_placed[1], NC // 2)
            for d in range(DT):
                act_h_hi(act, norms[0], 0, d)
                act_square(act, norms[0], 1, d)
            act_early_slot(act, 0, 2)
            act_rstd(act, norms[0], 1, bank[2], (norms[0].summed, 1))
            for d in range(DT):
                act_h_hi(act, norms[0], 1, d)
            act_early_slot(act, 0, 3)
            act_ffn(act, ffn_a)
            act_norm_after(act, norms[1], ffn_a.xadd, DT * (GROUPS - 1), MIX0)
            act_mixer(act)
            act_out(act, norms[2])
            act_ffn(act, ffn_b)
            act_norm_after(act, norms[3], ffn_b.xadd, DT * (GROUPS - 1), None)
            for t in ACT_PLACES:
                if t >= 4:
                    act.wait_ge(s_out[t % 4], 16)
                act.wait_ge(s_outturn, t + 1)
                act.activation(stage[:, t % 4], bank[t % 2][:], ACT.Copy).then_inc(s_placed_out[1], 1)

        @block.vector
        def _(dve):
            def place(t):
                dve.wait_ge(s_turned, t + 1)
                dve.tensor_copy(xT[:, :, t * P:(t + 1) * P],
                                bank[0][:].rearrange("p (d t) -> p d t", t=P)).then_inc(s_placed[0], 1)

            place(0)
            place(2)
            dve.wait_ge(s_vturn, 1)
            dve.tensor_copy(gains[:], bank[2][:, 0:NVEC]).then_inc(s_gains, 1)
            dve.wait_ge(s_gains, 1)
            l0, l1 = gains[:, V_LOGIT0:V_LOGIT1], gains[:, V_LOGIT1:V_HEAD]
            dve.tensor_tensor(lbv[:, L_MAX], l0, l1, ALU.max).then_inc(s_lb, 1)
            dve.wait_ge(s_lb, 1)
            dve.tensor_tensor(lbv[:, L_E0], l0, lbv[:, L_MAX], ALU.subtract).then_inc(s_lb, 1)
            dve.tensor_tensor(lbv[:, L_E1], l1, lbv[:, L_MAX], ALU.subtract).then_inc(s_lb, 1)
            place(4)
            place(6)
            dve.wait_ge(s_lbexp, 1)
            dve.tensor_tensor(lbv[:, L_SUM], lbv[:, L_E0], lbv[:, L_E1], ALU.add).then_inc(s_lb, 1)
            dve.wait_ge(s_lb, 4)
            dve.reciprocal(lbv[:, L_INV], lbv[:, L_SUM]).then_inc(s_lb, 1)
            dve.wait_ge(s_lb, 5)
            dve.tensor_tensor(lbv[:, L_LB], lbv[:, L_E0], lbv[:, L_INV], ALU.mult).then_inc(s_lb, 1)
            dve.wait_ge(s_lb, 6)
            dve.tensor_scalar(lbv[:, L_ONE_MINUS], lbv[:, L_LB], -1.0, 1.0, ALU.mult, ALU.add).then_inc(s_lb, 1)
            dve.tensor_scalar(lbv[:, L_MINUS], lbv[:, L_LB], 1.0, None, ALU.subtract).then_inc(s_lb, 1)
            dve.wait_ge(s_lb, 8)
            dve.tensor_scalar(lbv[:, L_LB], lbv[:, L_LB], TINY, None, ALU.max).then_inc(s_lb, 1)
            dve.wait_ge(s_lb, 9)
            for d in range(DT):
                dve_h_tile(dve, norms[0], 0, 0, d)
                if d:
                    dve_add_square(dve, norms[0], 1, d - 1)
            dve_add_square(dve, norms[0], 1, DT - 1)
            for d in range(DT):
                dve_h_tile(dve, norms[0], 0, 1, d)
            dve_ffn(dve, ffn_a, lambda c, d: dve_h_tile(dve, norms[1], 1, c, d))
            dve.wait_ge(s_ones, 1)
            dve.wait_ge(s_ident, 2)
            dve.wait_ge(s_mask, 2 * len(MASKS) + 1)
            dve_mixer(dve)
            dve_out(dve, norms[2], 2)

            def scale_turn(c, d):
                if c == 0 and d in (2, 3):
                    return
                if c == 0 and d in (4, 5):
                    d -= 2
                if d == 0:
                    dve.wait_ge(norms[3].rstd, c + 1)
                if d < DVE_SCALES[c]:
                    dve.scalar_tensor_tensor(out=xT[:, d, BOTH[c]], in0=xT[:, d, BOTH[c]],
                                             scalar=gains[:, V_FINAL + d:V_FINAL + d + 1],
                                             in1=rstd[:, BOTH[c]], op0=ALU.mult,
                                             op1=ALU.mult).then_inc(s_final[0], 1)

            dve_ffn(dve, ffn_b, scale_turn)
            for t in DVE_PLACES:
                dve.wait_ge(s_out[t % 4], 16)
                dve.wait_ge(s_outturn, t + 1)
                dve.tensor_copy(stage[:, t % 4], bank[t % 2][:]).then_inc(s_placed_out[0], 1)

        @block.tensor
        def _(pe):
            pe.wait_ge(s_ident, 2)
            for t in range(NC):
                if t == 4:
                    pe.wait_ge(s_vec, 64)
                    pe.transpose(bank[2][:, 0:NVEC], vec_rows[:], ident[0:NVEC, 0:NVEC]).then_inc(s_vturn, 1)
                pe.wait_ge(s_xload[t % 4], 16 * (t // 4 + 1))
                if t >= 2:
                    pe.wait_ge(s_placed[t % 2], t // 2)
                for d in range(DT):
                    mm = pe.transpose(bank[t % 2][:, d * P:(d + 1) * P], stage[:, t % 4, d * P:(d + 1) * P],
                                      ident[:])
                mm.then_inc(s_turned, 1)
                if t == 5:
                    pe.wait_ge(s_ones, 1)
                    pe.wait_ge(s_gains, 1)
                    pe_square_sum(pe, norms[0], bank[2], (0, 1))
                elif t == 6:
                    pe_square_sum(pe, norms[0], bank[2], (2, 3, 4))
                elif t == 7:
                    pe_square_sum(pe, norms[0], bank[2], (5, 6, 7))
            for placed in s_placed:
                pe.wait_ge(placed, NC // 2)
            pe_ffn(pe, ffn_a)
            pe_mixer(pe)
            for d in range(2, DT - 2):
                if d >= 4:
                    pe.wait_ge(o_add, d - 3)
                pe_col_unit(pe, OUT0 + d, d % 4, bank[d % 4])
            for c in range(2):
                for d in (DT - 2, DT - 1):
                    if c == 0:
                        pe.wait_ge(s_clo, OUT0 + d + 1)
                        pe.wait_ge(o_add, d - 3)
                    for k in range(DT):
                        mm = pe_col_tile(pe, d, k, bank[d % 4], (BOTH[c],))
                        if k == DT - 1:
                            mm.then_inc(o_last if c == 0 else s_cdone, 1)
                        if c == 1 and d == DT - 2 and k == 3:
                            pe_norm_sum(pe, norms[2], 0, bank[1])
            pe_ffn(pe, ffn_b)
            pe_norm_sum(pe, norms[3], 1, bank[2])
            for t in range(NC):
                if t >= 2:
                    wait_placed(pe, t - 2)
                for d in range(DT):
                    if t % 4 == 0:
                        by_dve = DVE_SCALES[t // 4]
                        if d < by_dve:
                            pe.wait_ge(s_final[0], (t // 4) * DVE_SCALES[0] + d + 1)
                        else:
                            pe.wait_ge(s_final[1], (t // 4) * (DT - DVE_SCALES[0]) + d - by_dve + 1)
                    mm = pe.transpose(bank[t % 2][:, d * P:(d + 1) * P], xT[:, d, t * P:(t + 1) * P],
                                      ident[:])
                mm.then_inc(s_outturn, 1)


_INS = ['x', 'ffn_w_gate_up', 'ffn_w_down', 'norm_gains', 'final_norm_gain', 'hgrn_w_in',
        'hgrn_lower_bound_logits', 'hgrn_norm_gain', 'hgrn_w_out']


def kernel(**inputs):
    import numpy as np
    import concourse.bacc as bacc
    from concourse.bass_utils import run_bass_kernel_spmd

    nc = bacc.Bacc("TRN2", target_bir_lowering=False, num_devices=1)
    arrays, args = {}, []
    for name in _INS:
        a = np.ascontiguousarray(inputs[name])
        arrays[f"in_{name}"] = a
        args.append(nc.dram_tensor(f"in_{name}", a.shape, mybir.dt.from_np(a.dtype), kind="ExternalInput").ap())
    args.append(nc.dram_tensor("trunk_out", (1, T, D), F32, kind="ExternalOutput").ap())
    hgrn2_trunk(nc, *args)
    r = run_bass_kernel_spmd(nc, [arrays], core_ids=[0])
    return r.results[0]["trunk_out"]
```
